# Optimizing a Trainium2 kernel written in Bass

```python
import math
import jax, jax.numpy as jnp
from jax import lax
import numpy as np

D_MODEL = 1024
BATCH = 1
SEQ = 128
DEPTH = 1
DEC_BATCH = 1
DEC_SEQ = 1024
PAST_LEN = 128

GRID_W = 64
HEAD_DIM = 64
D_MIX = D_MODEL
D_M = D_MIX // 4
H_M = D_M // HEAD_DIM
DK = HEAD_DIM
DV = HEAD_DIM
D_S = 3 * D_MIX // 8
H_S = D_S // HEAD_DIM
P_S = HEAD_DIM
G_S = 2
R_S = H_S // G_S
N_S = 64
D_XBC = D_S + 2 * G_S * N_S
CONV_K = 3
D_NA = D_MIX - D_M - D_S
H_NA = D_NA // HEAD_DIM
WIN_H = 8
WIN_W = 16
Q_COLS = 16
K_COLS = 2 * WIN_W
Q_BLOCK = 128
CHUNK = 64
N_EXPERTS = 16
EC_FACTOR = 2
D_FF = 1024
EPS = 1e-6
NEG_INIT = -1e30
SECTIONS = (D_M, D_M, D_M, D_M, 2 * H_M, 2 * H_M, D_S, D_XBC, 2 * H_S, D_NA, D_NA, D_NA)

kernel_name = 'hybrid_mlstm_ssd_natten_ec_dit'

def rmsnorm(x, g):
    xf = x.astype(jnp.float32)
    y = xf * lax.rsqrt(jnp.mean(xf * xf, axis=-1, keepdims=True) + EPS)
    return (y * g.astype(jnp.float32)).astype(x.dtype)

def modulate(x, g, shift, scale):
    return rmsnorm(x, g) * (1.0 + scale) + shift

def project(h, w_in):
    points = np.cumsum(SECTIONS)[:-1].tolist()
    return jnp.split(h @ w_in, points, axis=-1)

def depthwise_conv(x, w, b):
    ch = x.shape[-1]
    y = lax.conv_general_dilated(x, w[:, None, :].astype(x.dtype), window_strides=(1,),
                                 padding=[(CONV_K // 2, CONV_K // 2)],
                                 dimension_numbers=('NWC', 'WIO', 'NWC'), feature_group_count=ch)
    return y + b.astype(x.dtype)

def mlstm_chunked(q, k, v, ig, logf, C0, n0, m0):
    B, H, T, _ = q.shape
    nc = T // CHUNK

    def to_chunks(a):
        return jnp.moveaxis(a.reshape(a.shape[:2] + (nc, CHUNK) + a.shape[3:]), 2, 0)

    xs = (to_chunks(q), to_chunks(k), to_chunks(v), to_chunks(ig), to_chunks(logf))
    causal = jnp.tril(jnp.ones((CHUNK, CHUNK), dtype=bool))

    def step(carry, xc):
        C, n, m = carry
        qc, kc, vc, ic, fc = xc
        b = jnp.cumsum(fc, axis=-1)
        logD = jnp.where(causal, b[..., :, None] - b[..., None, :] + ic[..., None, :], -jnp.inf)
        m_inter = b + m[..., None]
        m_t = jnp.maximum(jnp.max(logD, axis=-1), m_inter)
        dmat = jnp.exp(logD - m_t[..., None])
        w_inter = jnp.exp(m_inter - m_t)
        s = jnp.einsum('bhtd,bhsd->bhts', qc, kc) * dmat
        num = jnp.einsum('bhts,bhsv->bhtv', s, vc) + w_inter[..., None] * jnp.einsum('bhtd,bhdv->bhtv', qc, C)
        den = jnp.sum(s, axis=-1) + w_inter * jnp.einsum('bhtd,bhd->bht', qc, n)
        h = num / jnp.maximum(jnp.abs(den), jnp.exp(-m_t))[..., None]
        bL = b[..., -1]
        lw = bL[..., None] - b + ic
        m_new = jnp.maximum(bL + m, jnp.max(lw, axis=-1))
        wk = jnp.exp(lw - m_new[..., None])
        decay = jnp.exp(bL + m - m_new)
        C_new = decay[..., None, None] * C + jnp.einsum('bhs,bhsd,bhsv->bhdv', wk, kc, vc)
        n_new = decay[..., None] * n + jnp.einsum('bhs,bhsd->bhd', wk, kc)
        return (C_new, n_new, m_new), h

    final, hs = lax.scan(step, (C0, n0, m0), xs)
    h = jnp.moveaxis(hs, 0, 2).reshape(B, H, T, -1)
    return h, final

def mlstm_mixer(mq, mk, mv, mo, mi, mf, f_bias, norm_g, C0, n0, m0):
    B, T, _ = mq.shape
    f32 = jnp.float32

    def heads(a):
        return a.reshape(B, T, H_M, -1).transpose(0, 2, 1, 3).astype(f32)

    q = heads(mq)
    k = heads(mk) * (DK ** -0.5)
    v = heads(mv)
    ig = mi.reshape(B, T, 2, H_M).astype(f32).transpose(2, 0, 3, 1)
    logf = jax.nn.log_sigmoid(mf.reshape(B, T, 2, H_M).astype(f32) + f_bias.astype(f32)).transpose(2, 0, 3, 1)
    C0 = C0.astype(f32)
    n0 = n0.astype(f32)
    m0 = m0.astype(f32)
    hf, sf = mlstm_chunked(q, k, v, ig[0], logf[0], C0[:, 0], n0[:, 0], m0[:, 0])
    fl = lambda a: jnp.flip(a, axis=2)
    hb, sb = mlstm_chunked(fl(q), fl(k), fl(v), fl(ig[1]), fl(logf[1]), C0[:, 1], n0[:, 1], m0[:, 1])
    h = (hf + fl(hb)).transpose(0, 2, 1, 3)
    h = h * lax.rsqrt(jnp.mean(h * h, axis=-1, keepdims=True) + EPS)
    h = h.reshape(B, T, D_M) * norm_g.astype(f32) * jax.nn.sigmoid(mo.astype(f32))
    C_fin = jnp.stack([sf[0], sb[0]], axis=1)
    n_fin = jnp.stack([sf[1], sb[1]], axis=1)
    m_fin = jnp.stack([sf[2], sb[2]], axis=1)
    return h.astype(mq.dtype), C_fin, n_fin, m_fin

def ssd_chunked(x, dt, A, Bm, Cm, h0):
    B, T = x.shape[:2]
    nc = T // CHUNK

    def to_chunks(a):
        return jnp.moveaxis(a.reshape((B, nc, CHUNK) + a.shape[2:]), 1, 0)

    xs = (to_chunks(x), to_chunks(dt), to_chunks(Bm), to_chunks(Cm))
    causal = jnp.tril(jnp.ones((CHUNK, CHUNK), dtype=bool))

    def step(h, xc):
        xq, dtc, Bc, Cc = xc
        a = jnp.cumsum(dtc * A, axis=1)
        at = jnp.moveaxis(a, 1, -1)
        seg = jnp.exp(jnp.where(causal, at[..., :, None] - at[..., None, :], -jnp.inf))
        cb = jnp.einsum('btgn,bsgn->bgts', Cc, Bc)
        y = jnp.einsum('bgts,bgrts,bsgr,bsgrp->btgrp', cb, seg, dtc, xq)
        y = y + jnp.einsum('btgn,bgrpn->btgrp', Cc, h) * jnp.exp(a)[..., None]
        aL = a[:, -1]
        wk = jnp.exp(aL[:, None] - a) * dtc
        h_new = jnp.exp(aL)[..., None, None] * h + jnp.einsum('bsgr,bsgrp,bsgn->bgrpn', wk, xq, Bc)
        return h_new, y

    hT, ys = lax.scan(step, h0, xs)
    y = jnp.moveaxis(ys, 0, 1).reshape(x.shape)
    return y, hT

def ssm_mixer(sz, sxbc, sdt, conv_w, conv_b, dt_bias, a_log, d_skip, norm_g, h0):
    B, T, _ = sxbc.shape
    f32 = jnp.float32
    xbc = jax.nn.silu(depthwise_conv(sxbc, conv_w, conv_b))
    xs, Bm, Cm = jnp.split(xbc, [D_S, D_S + G_S * N_S], axis=-1)
    x = xs.reshape(B, T, G_S, R_S, P_S).astype(f32)
    Bm = Bm.reshape(B, T, G_S, N_S).astype(f32)
    Cm = Cm.reshape(B, T, G_S, N_S).astype(f32)
    dt = jax.nn.softplus(sdt.reshape(B, T, 2, H_S).astype(f32) + dt_bias.astype(f32)).reshape(B, T, 2, G_S, R_S)
    A = -jnp.exp(a_log.astype(f32)).reshape(2, G_S, R_S)
    h0 = h0.astype(f32).reshape(B, 2, G_S, R_S, P_S, N_S)
    yf, hf = ssd_chunked(x, dt[:, :, 0], A[0], Bm, Cm, h0[:, 0])
    fl = lambda a: jnp.flip(a, axis=1)
    yb, hb = ssd_chunked(fl(x), fl(dt[:, :, 1]), A[1], fl(Bm), fl(Cm), h0[:, 1])
    y = yf + fl(yb) + d_skip.astype(f32).reshape(G_S, R_S)[:, :, None] * x
    y = y.reshape(B, T, D_S) * jax.nn.silu(sz.astype(f32))
    y = rmsnorm(y, norm_g)
    hT = jnp.stack([hf, hb], axis=1).reshape(B, 2, H_S, P_S, N_S)
    return y.astype(sz.dtype), hT

def ctx_self_attention(q, k, v):
    B, L, H, d = q.shape
    nb = L // Q_BLOCK
    qb = jnp.moveaxis(q.reshape(B, nb, Q_BLOCK, H, d), 1, 0)
    scale = d ** -0.5

    def block(qi):
        s = jnp.einsum('bqhd,bkhd->bhqk', qi, k).astype(jnp.float32) * scale
        p = jax.nn.softmax(s, axis=-1).astype(v.dtype)
        return jnp.einsum('bhqk,bkhd->bqhd', p, v)

    o = lax.map(block, qb)
    return jnp.moveaxis(o, 0, 1).reshape(B, L, H * d)

def latent_neighbourhood_attention(q, k, v, ck, cv, rpb):
    B, T, H, d = q.shape
    rows = T // GRID_W
    kh = min(WIN_H, rows)
    ncb = GRID_W // Q_COLS
    j = np.arange(ncb)
    qcol = j[:, None] * Q_COLS + np.arange(Q_COLS)[None, :]
    kstart = np.clip(j * Q_COLS - WIN_W // 2, 0, GRID_W - K_COLS)
    kcol = kstart[:, None] + np.arange(K_COLS)[None, :]
    cstart = np.clip(qcol - WIN_W // 2, 0, GRID_W - WIN_W)
    col_ok = (kcol[:, None, :] >= cstart[:, :, None]) & (kcol[:, None, :] < cstart[:, :, None] + WIN_W)
    col_off = np.clip(kcol[:, None, :] - qcol[:, :, None] + WIN_W - 1, 0, 2 * WIN_W - 2)
    rpb_cols = rpb[:, :, col_off]
    col_ok = jnp.asarray(col_ok)[:, :, None, :]
    kg = k.reshape(B, rows, GRID_W, H, d)
    vg = v.reshape(B, rows, GRID_W, H, d)
    qg = jnp.moveaxis(q.reshape(B, rows, ncb, Q_COLS, H, d), 1, 0)
    scale = d ** -0.5
    n_loc = kh * K_COLS

    def row_block(args):
        r, qr = args
        rs = jnp.clip(r - kh // 2, 0, rows - kh)
        kr = lax.dynamic_slice_in_dim(kg, rs, kh, axis=1)[:, :, kcol]
        vr = lax.dynamic_slice_in_dim(vg, rs, kh, axis=1)[:, :, kcol]
        s_loc = jnp.einsum('bjqhd,bkjchd->bhjqkc', qr, kr).astype(jnp.float32) * scale
        row_off = rs + jnp.arange(kh) - r + WIN_H - 1
        bias = jnp.transpose(jnp.take(rpb_cols, row_off, axis=1), (0, 2, 3, 1, 4)).astype(jnp.float32)
        s_loc = jnp.where(col_ok, s_loc + bias, -jnp.inf).reshape(B, H, ncb, Q_COLS, n_loc)
        s_ctx = jnp.einsum('bjqhd,blhd->bhjql', qr, ck).astype(jnp.float32) * scale
        p = jax.nn.softmax(jnp.concatenate([s_loc, s_ctx], axis=-1), axis=-1).astype(v.dtype)
        p_loc = p[..., :n_loc].reshape(B, H, ncb, Q_COLS, kh, K_COLS)
        p_ctx = p[..., n_loc:]
        o = jnp.einsum('bhjqkc,bkjchd->bjqhd', p_loc, vr) + jnp.einsum('bhjql,blhd->bjqhd', p_ctx, cv)
        return o.reshape(B, GRID_W, H, d)

    o = lax.map(row_block, (jnp.arange(rows), qg))
    return jnp.moveaxis(o, 0, 1).reshape(B, T, H * d)

def token_mixer_context(h, w_in, f_bias, m_norm_g, conv_w, conv_b, dt_bias, a_log, d_skip, s_norm_g, w_out):
    B, L, _ = h.shape
    mq, mk, mv, mo, mi, mf, sz, sxbc, sdt, nq, nk, nv = project(h, w_in)
    C0 = jnp.zeros((B, 2, H_M, DK, DV), jnp.float32)
    n0 = jnp.zeros((B, 2, H_M, DK), jnp.float32)
    m0 = jnp.full((B, 2, H_M), NEG_INIT, jnp.float32)
    m_out, C, n, m = mlstm_mixer(mq, mk, mv, mo, mi, mf, f_bias, m_norm_g, C0, n0, m0)
    h0 = jnp.zeros((B, 2, H_S, P_S, N_S), jnp.float32)
    s_out, hs = ssm_mixer(sz, sxbc, sdt, conv_w, conv_b, dt_bias, a_log, d_skip, s_norm_g, h0)
    q = nq.reshape(B, L, H_NA, HEAD_DIM)
    k = nk.reshape(B, L, H_NA, HEAD_DIM)
    v = nv.reshape(B, L, H_NA, HEAD_DIM)
    a_out = ctx_self_attention(q, k, v)
    y = jnp.concatenate([m_out, s_out, a_out], axis=-1) @ w_out
    return y, k, v, C, n, m, hs

def token_mixer_latent(h, ck, cv, C0, n0, m0, h0, w_in, f_bias, m_norm_g, conv_w, conv_b, dt_bias, a_log,
                       d_skip, s_norm_g, rpb, w_out):
    B, T, _ = h.shape
    mq, mk, mv, mo, mi, mf, sz, sxbc, sdt, nq, nk, nv = project(h, w_in)
    m_out, _, _, _ = mlstm_mixer(mq, mk, mv, mo, mi, mf, f_bias, m_norm_g, C0, n0, m0)
    s_out, _ = ssm_mixer(sz, sxbc, sdt, conv_w, conv_b, dt_bias, a_log, d_skip, s_norm_g, h0)
    q = nq.reshape(B, T, H_NA, HEAD_DIM)
    k = nk.reshape(B, T, H_NA, HEAD_DIM)
    v = nv.reshape(B, T, H_NA, HEAD_DIM)
    a_out = latent_neighbourhood_attention(q, k, v, ck.astype(q.dtype), cv.astype(v.dtype), rpb)
    return jnp.concatenate([m_out, s_out, a_out], axis=-1) @ w_out

def ec_moe(h, router_w, w1, w3, w2):
    B, T, D = h.shape
    xt = h.reshape(B * T, D)
    cap = EC_FACTOR * (B * T) // N_EXPERTS
    aff = jax.nn.softmax((xt @ router_w).astype(jnp.float32), axis=-1)
    gate_vals, idx = lax.top_k(aff.T, cap)
    xe = xt[idx]
    hid = jax.nn.silu(jnp.einsum('ecd,edf->ecf', xe, w1)) * jnp.einsum('ecd,edf->ecf', xe, w3)
    ye = jnp.einsum('ecf,efd->ecd', hid, w2) * gate_vals[..., None]
    y = jnp.zeros_like(xt).at[idx.reshape(-1)].add(ye.reshape(-1, D).astype(xt.dtype))
    return y.reshape(B, T, D)

def setup_inputs(seed: int = 0) -> dict:
    key = jax.random.key(seed)
    ks = jax.random.split(key, 32)
    f32 = jnp.float32
    nrm = lambda kk, shp: jax.random.normal(kk, shp, f32)
    D = D_MODEL
    return {
        'x_prompt': nrm(ks[0], (BATCH, SEQ, D)),
        'x_sample': nrm(ks[1], (DEC_BATCH, DEC_SEQ, D)),
        'cache_na_k': nrm(ks[2], (DEC_BATCH, DEPTH, PAST_LEN, H_NA, HEAD_DIM)),
        'cache_na_v': nrm(ks[3], (DEC_BATCH, DEPTH, PAST_LEN, H_NA, HEAD_DIM)),
        'state_mlstm_c': 0.5 * nrm(ks[4], (DEC_BATCH, DEPTH, 2, H_M, DK, DV)),
        'state_mlstm_n': nrm(ks[5], (DEC_BATCH, DEPTH, 2, H_M, DK)),
        'state_mlstm_m': nrm(ks[6], (DEC_BATCH, DEPTH, 2, H_M)),
        'state_ssm': 0.5 * nrm(ks[7], (DEC_BATCH, DEPTH, 2, H_S, P_S, N_S)),
        'c': nrm(ks[8], (DEC_BATCH, D)),
        'c_ctx': nrm(ks[9], (D,)),
        'ada_w': 0.5 * D ** -0.5 * nrm(ks[10], (DEPTH, D, 6 * D)),
        'ada_b': 0.02 * nrm(ks[11], (DEPTH, 6 * D)),
        'norm1_g': 1.0 + 0.05 * nrm(ks[12], (DEPTH, D)),
        'norm2_g': 1.0 + 0.05 * nrm(ks[13], (DEPTH, D)),
        'w_in': D ** -0.5 * nrm(ks[14], (DEPTH, D, sum(SECTIONS))),
        'mlstm_f_bias': 3.0 + 0.5 * nrm(ks[15], (DEPTH, 2, H_M)),
        'mlstm_norm_g': 1.0 + 0.05 * nrm(ks[16], (DEPTH, D_M)),
        'conv_w': CONV_K ** -0.5 * nrm(ks[17], (DEPTH, CONV_K, D_XBC)),
        'conv_b': 0.02 * nrm(ks[18], (DEPTH, D_XBC)),
        'ssm_dt_bias': -3.0 + 0.5 * nrm(ks[19], (DEPTH, 2, H_S)),
        'ssm_a_log': jnp.log(jax.random.uniform(ks[20], (DEPTH, 2, H_S), f32, 1.0, 16.0)),
        'ssm_d': 1.0 + 0.1 * nrm(ks[21], (DEPTH, H_S)),
        'ssm_norm_g': 1.0 + 0.05 * nrm(ks[22], (DEPTH, D_S)),
        'na_rpb': 0.1 * nrm(ks[23], (DEPTH, H_NA, 2 * WIN_H - 1, 2 * WIN_W - 1)),
        'w_out': D_MIX ** -0.5 * nrm(ks[24], (DEPTH, D_MIX, D)),
        'router_w': D ** -0.5 * nrm(ks[25], (DEPTH, D, N_EXPERTS)),
        'exp_w1': D ** -0.5 * nrm(ks[26], (DEPTH, N_EXPERTS, D, D_FF)),
        'exp_w3': D ** -0.5 * nrm(ks[27], (DEPTH, N_EXPERTS, D, D_FF)),
        'exp_w2': D_FF ** -0.5 * nrm(ks[28], (DEPTH, N_EXPERTS, D_FF, D)),
        'final_g': 1.0 + 0.05 * nrm(ks[29], (D,)),
    }

def reference(x_prompt, x_sample, cache_na_k, cache_na_v, state_mlstm_c, state_mlstm_n, state_mlstm_m,
              state_ssm, c, c_ctx, ada_w, ada_b, norm1_g, norm2_g, w_in, mlstm_f_bias, mlstm_norm_g,
              conv_w, conv_b, ssm_dt_bias, ssm_a_log, ssm_d, ssm_norm_g, na_rpb, w_out, router_w,
              exp_w1, exp_w3, exp_w2, final_g):
    xp = x_prompt
    xs = x_sample
    ks, vs, cs, ns, ms, hs = [], [], [], [], [], []
    for l in range(DEPTH):
        mod = jax.nn.silu(c_ctx) @ ada_w[l] + ada_b[l]
        sh1, sc1, g1, sh2, sc2, g2 = jnp.split(mod, 6, axis=-1)
        y, k_l, v_l, c_l, n_l, m_l, h_l = token_mixer_context(
            modulate(xp, norm1_g[l], sh1, sc1), w_in[l], mlstm_f_bias[l], mlstm_norm_g[l], conv_w[l],
            conv_b[l], ssm_dt_bias[l], ssm_a_log[l], ssm_d[l], ssm_norm_g[l], w_out[l])
        xp = xp + g1 * y
        xp = xp + g2 * ec_moe(modulate(xp, norm2_g[l], sh2, sc2), router_w[l], exp_w1[l], exp_w3[l], exp_w2[l])
        ks.append(k_l)
        vs.append(v_l)
        cs.append(c_l)
        ns.append(n_l)
        ms.append(m_l)
        hs.append(h_l)
        mod = (jax.nn.silu(c) @ ada_w[l] + ada_b[l])[:, None, :]
        sh1, sc1, g1, sh2, sc2, g2 = jnp.split(mod, 6, axis=-1)
        y = token_mixer_latent(
            modulate(xs, norm1_g[l], sh1, sc1), cache_na_k[:, l], cache_na_v[:, l], state_mlstm_c[:, l],
            state_mlstm_n[:, l], state_mlstm_m[:, l], state_ssm[:, l], w_in[l], mlstm_f_bias[l],
            mlstm_norm_g[l], conv_w[l], conv_b[l], ssm_dt_bias[l], ssm_a_log[l], ssm_d[l], ssm_norm_g[l],
            na_rpb[l], w_out[l])
        xs = xs + g1 * y
        xs = xs + g2 * ec_moe(modulate(xs, norm2_g[l], sh2, sc2), router_w[l], exp_w1[l], exp_w3[l], exp_w2[l])
    y_prompt = rmsnorm(xp, final_g)
    y_sample = rmsnorm(xs, final_g)
    new_na_k = jnp.stack(ks, axis=1)
    new_na_v = jnp.stack(vs, axis=1)
    new_mlstm_c = jnp.stack(cs, axis=1)
    new_mlstm_n = jnp.stack(ns, axis=1)
    new_mlstm_m = jnp.stack(ms, axis=1)
    new_ssm = jnp.stack(hs, axis=1)
    return (y_prompt, y_sample, new_na_k, new_na_v, new_mlstm_c, new_mlstm_n, new_mlstm_m, new_ssm)


_drawn_inputs = setup_inputs


def setup_inputs(seed=0):
    import zlib

    import numpy as np

    out = dict(_drawn_inputs(seed))
    spreads = {}
    factors = {'cache_na_k': 4.646,
     'cache_na_v': 3.939,
     'state_mlstm_c': 8.0,
     'state_mlstm_n': 8.0,
     'state_mlstm_m': 8.0,
     'state_ssm': 5.868,
     'norm2_g': 5.594,
     'mlstm_norm_g': 8.0,
     'ssm_d': 8.0,
     'ssm_norm_g': 5.587,
     'na_rpb': 64.0}
    for name, (base, spread) in spreads.items():
        noise = np.random.default_rng([zlib.crc32(name.encode()), seed]).standard_normal(out[name].shape)
        drawn = base * np.exp(spread * noise) if base else spread * noise
        out[name] = __import__('jax').numpy.asarray(drawn.astype(out[name].dtype))
    for name, factor in factors.items():
        out[name] = (out[name] * factor).astype(out[name].dtype)
    return out
```

```python
from contextlib import ExitStack

import concourse.bass as bass
from concourse import mybir

F32 = mybir.dt.float32
I32 = mybir.dt.int32
U32 = mybir.dt.uint32
ALU = mybir.AluOpType
ACT = mybir.ActivationFunctionType
AX = mybir.AxisListType.X

P = 128
D = 1024
KD = D // P
NT = 9
NL = NT - 1
T = NT * P
HD = 64
HM, HS, HN = 4, 6, 6
GS, RS = 2, 3
NE = 16
CAPL, CAPC = 2 * NL * P // NE, 2 * P // NE
SLOTS = CAPL + CAPC
EPS = 1e-6
NEG = -1e30
SCALE = HD ** -0.5
GRID = 64
GW = 64
NDIR = 2

C_Q, C_K, C_V, C_O, C_G, C_Z, C_X, C_DT, C_NQ, C_NK, C_NV = 0, 256, 512, 768, 1024, 1040, 1424, 2064, 2076, 2460, 2844
C_END = 3228
SLAB = 256
RING = 4
ARENA = 44600

V_C, V_ADAB, V_N1, V_N2, V_MG, V_SG, V_CB, V_CW, V_END = 0, 16, 64, 72, 80, 82, 85, 90, 105
R_FB, R_DTB, R_ALOG, R_D, R_M0, R_END = 0, 8, 20, 32, 38, 46


def plan_slabs():
    ada = [("ada", m * SLAB, SLAB) for m in range(24)]
    first = [(C_Q, 256), (C_K, 256), (C_V, 256), (C_O, 256), (C_G, 256), (C_G + 256, 144),
             (C_X, 256), (C_X + 256, 256), (C_X + 512, 140)]
    second = [(C_NQ, 256), (C_NQ + 256, 256), (C_NQ + 512, 256), (C_NV, 256), (C_NV + 256, 128)]
    win1 = [("win", a, n) for a, n in first]
    win2 = [("win", a, n) for a, n in second]
    wout = [("wout", j * SLAB, SLAB) for j in range(4)]
    return ada[:8] + win1 + win2 + ada[8:] + wout


def plan_groups():
    g = []

    def t_block(slab, col, target, engines="ADA"):
        for t3 in range(3):
            g.append(("T", slab, col, 128, t3, target, engines[t3]))

    def rows(slab, col, n, target, engine):
        for i in range(NT):
            g.append(("R", slab, col, n, i, target, engine))

    def turn(src, target):
        for t3 in range(3):
            g.append(("X", None, 0, 384, t3, (src, target), "DAD"[t3]))

    for b in range(2):
        t_block(8, 128 * b, ("qT", b))
    for b in range(2):
        t_block(9, 128 * b, ("kT", b), "DAD")
    rows(10, 0, 256, ("v",), "D")
    rows(11, 0, 256, ("mo",), "A")
    for b in range(2):
        turn(("kT", b), ("krows", b))
    rows(12, 0, 256, ("gz",), "A")
    rows(13, 0, 144, ("z2",), "A")
    for b in range(5):
        t_block(14 + b // 2, 128 * (b % 2), ("raw", b), "DDD")
        g.append(("C", None, 0, 0, 0, ("conv", b), "B"))
        if b >= 1:
            turn(("conv", b - 1), ("xrows", b - 1))
    for t3 in range(3):
        g.append(("T", 16, 128, 2 * HS, t3, ("dtT", 0), "D"))
    for t3 in range(3):
        g.append(("X", None, 0, 6 * HS, t3, (("dtT", 0), ("dt", 0)), "D"))
    n_first = len(g)
    for b in range(3):
        t_block(17 + b // 2, 128 * (b % 2), ("nqT", b), "AAA")
    for b in range(3):
        t_block(17 + (3 + b) // 2, 128 * ((3 + b) % 2), ("nkT", b), "AAA")
    rows(20, 0, 256, ("nv", 0), "A")
    rows(21, 0, 128, ("nv", 256), "A")
    return g, n_first


def hybrid_layer(nc, x_prompt, x_sample, cacheT_k, cache_v, state_c, state_n, state_m, state_sT, c, c_ctx, ada_w, ada_b,
                 norm1_g, norm2_g, w_in, f_bias, m_norm_g, conv_w, conv_b, dt_bias, a_log, d_skip, s_norm_g, rpb_pad,
                 w_out, router_w, exp_w1, exp_w3, exp_w2, final_g,
                 y_prompt, y_sample, new_kT, new_v, new_c, new_n, new_m, new_sT):
    slabs = plan_slabs()
    groups, n_first = plan_groups()
    pe_groups = [g for g in groups if g[0] != "C"]
    pe_index = {n: i for i, n in enumerate(n for n, g in enumerate(groups) if g[0] != "C")}

    counts = {"A": [0], "D": [0]}
    for g in groups:
        for e in "AD":
            counts[e].append(counts[e][-1] + (g[0] != "C" and g[6] == e))

    def evacuated(engine, n):
        return counts[engine][n]

    def last_of(target):
        return max(n for n, g in enumerate(groups) if g[5] == target)

    G1, WOUT = 22, 38
    w_in_v = w_in.rearrange("(k p) n -> p k n", p=P)
    ada_v = ada_w.rearrange("(k p) n -> p k n", p=P)
    wout_v = w_out.rearrange("(k p) n -> p k n", p=P)
    w_src = {"ada": ada_v, "win": w_in_v, "wout": wout_v}

    def dram(name, shape):
        return nc.dram_tensor(name, shape, F32, kind="Internal").ap()

    mo_d, z_d = dram("mo_sigmoid", (T, 256)), dram("z_silu", (T, 384))
    h2c_d, h2l_d = dram("h2_context", (P, D)), dram("h2_latent", (NL * P, D))
    accc_d, accl_d = dram("moe_context", (P, D)), dram("moe_latent", (NL * P, D))

    with ExitStack() as ctx:
        def sb(name, shape, dt=F32):
            return ctx.enter_context(nc.sbuf_tensor(name, shape, dt))

        def sem(name):
            return ctx.enter_context(nc.semaphore(name))

        psum = ctx.enter_context(nc.psum_tensor("psum", [P, 8 * 512], F32))
        bk = [psum[:, 512 * i:512 * i + 512] for i in range(8)]

        ident, ones = sb("ident", [P, P]), sb("ones", [P, P])
        upto, downto = sb("upto", [P, P]), sb("downto", [P, P])
        mask = [sb("mask_f", [P, P]), sb("mask_b", [P, P])]
        vecs, vcol = sb("vecs", [P, P]), sb("vcol", [P, V_END])
        scol = sb("scol", [P, 16])
        smalls, smb = sb("smalls", [1, R_END]), sb("smb", [P, R_END])
        mrow, brow = sb("mrow", [2, 2, SLAB]), sb("brow", [1, 2, SLAB])
        modcol = sb("modcol", [P, 48, 2])
        gs = [sb("gs1", [P, KD, 2]), sb("gs2", [P, KD, 2])]
        sumsq, rstd = sb("sumsq", [P, 4, NT]), sb("rstd", [P, 4, NT])
        half = sb("half", [P, 36])
        G, dtr = sb("G", [P, NT, 16]), sb("dtr", [P, NT, 12])
        gt = sb("gt", [P, 25, 2 * GW])
        dec2 = sb("dec2", [P, NDIR, 2 * NT])
        Cst = sb("Cst", [P, 4, 2, 2, HD + 1])
        Hst = sb("Hst", [P, 4, GS, RS * HD])
        small = sb("small", [P, 2, 64])

        A = sb("arena", [P, ARENA])

        def view(off, *shape):
            n = 1
            for s in shape:
                n *= s
            assert off + n <= ARENA
            v = A[:, off:off + n]
            names = "abcd"[:len(shape)]
            if len(shape) == 1:
                return v
            return v.rearrange(f"p ({' '.join(names)}) -> p {' '.join(names)}", **dict(zip(names[1:], shape[1:])))

        R_RING, R_HT = 0, RING * KD * SLAB
        R_M = R_HT + KD * T
        R_S = R_M + 11556
        R_Y = R_S + 6916
        R_MM = R_Y + 3456
        R_SC = R_MM + 2304
        ring = view(R_RING, RING, KD, SLAB)
        hT = view(R_HT, KD, T)
        X = view(R_M, NT, D)
        qT, kT = view(R_M, 2, T), view(R_M + 2304, 2, T)
        krows = view(R_M + 4608, NT, 256)
        v1 = view(R_M + 6912, NT, HM, HD + 1)
        hacc = view(R_M + 9252, NT, HM, HD)
        BC = view(R_S, 2, T + 2)
        xrows = view(R_S + 2308, NT, 384)
        brows = view(R_S + 5764, NT, 128)
        yacc = view(R_Y, NT, 384)
        mixM = view(R_MM, 2, T)
        dtT = view(R_MM, T)
        mixA = view(R_Y, 3, T)
        raw = view(R_Y + 1024, 2, T + 4)
        cvx = view(R_SC, 2, T + 2)
        stage = view(R_Y, 4, 256)
        sq_junk = view(R_SC, 2, D)
        wkv = view(R_SC, 2, HM, HD + 1)
        Lm = view(R_SC + 520, 2, 2, 2, P)
        num = view(R_SC + 1544, 2, HM, HD + 1)
        rec = view(R_SC + 2064, 2, HM)
        htmp = view(R_SC + 2080, HM, HD)
        SQ = view(R_M + 4608, NT * HM, HD)
        mo = view(R_Y, NT, 256)
        Ls = view(R_SC, 2, GS, RS, P)
        xdt = view(R_SC + 1536, 2, HS, HD)
        hs = view(R_SC + 2304, RS * HD)
        wkx = view(R_M + 10368, 2, HS, HD)
        yint = view(R_M + 11136, HS, HD)
        z = view(R_S, NT, 384)
        mixS = view(R_S + 3460, 3, T)
        tb = view(R_HT, 2, 14, GRID)
        ti = view(R_HT + 1792, 2, 9, GRID)
        sc_sb = view(R_HT + 2944, 2, 704)
        pT = view(R_HT + 4352, 2, 6, P)
        ckT = view(R_HT + 5888, 3, P)
        cv = view(R_HT + 6272, 384)
        nmax, ssum, rsum = (view(R_HT + 6656 + 64 * i, 64) for i in range(3))
        xt, tw, nrow, h2T = (view(R_HT + 2048 * i, 2, D) for i in range(4))
        sq2 = view(R_HT + 8192, D)
        rw = view(R_SC + 2200, KD, NE)
        lg, aff = view(R_SC + 2336, NT, NE), view(R_SC + 2480, NT, NE)
        smx, ssm = view(R_SC + 2624, NT), view(R_SC + 2640, NT)
        g1b = view(R_SC, 2, D)
        g2b = view(R_M + 9216, 2, D)
        x1 = view(R_M, NT, D)
        affT = view(R_SC, T)
        vals, idxf = view(R_SC + 1152, SLOTS), view(R_SC + 1440, SLOTS)
        idxu = view(R_SC + 1296, SLOTS).bitcast(U32)
        R_E = R_S + 8192
        wslot = [view(4096 * i, KD, 512) for i in range(4)] + [view(R_S, KD, 512), view(R_S + 4096, KD, 512)]
        ye, xg = view(R_E, D), view(R_E + 1024, D)
        xeT, hid, yT = (view(R_E + 2048 + 1152 * i, KD, SLOTS) for i in range(3))
        gflat = gt[:, :, :].rearrange("p a b -> p (a b)")
        xgc, yec, sil = gflat[:, 0:1024], gflat[:, 1024:2048], gflat[:, 2048:2336].rearrange("p (a b) -> p a b", a=2)
        zero = gflat[:, 0:1024]
        R_I = R_SC + 2100
        gl, gc = view(R_I, NE), view(R_I + 16, NE)
        il, ic = view(R_I + 32, NE + 1).bitcast(I32), view(R_I + 49, NE + 1).bitcast(I32)
        gcur = view(R_I + 66, 2)
        icur = view(R_I + 68, 4).bitcast(I32)
        y9, fgb, sq3 = view(0, NT, D), view(9216, D), view(10240, 2, D)
        nqT, nkT = view(R_M, 3, T), view(R_M + 3456, 3, T)
        nv = view(R_M + 6912, NT, 384)

        def conv_out(b):
            return cvx[:, b % 2, :] if b < 3 else BC[:, b - 3, :]

        def cv_tok(i):
            return 0 if i == 0 else i * P + 2

        (FL, FE, F, IG, AC, AR, CMR, CMC, MX, MP, MN, NM, NMR, WINT, EMT, WKM, DEC,
         DT, DTE, DA, SA, SAR, SEA, SWK, SEL) = range(25)

        def gate(t, d=None, heads=HM):
            v = gt[:, t, :]
            if d is None:
                return v
            return v[:, d * GW:d * GW + NT * heads].rearrange("p (c h) -> p c h", h=heads)

        def gcol(t, d, c, h, heads=HM):
            i = d * GW + c * heads + h
            return gt[:, t, i:i + 1]

        def bc(ap, n):
            return ap.unsqueeze(len(ap.shape)).to_broadcast(list(ap.shape) + [n])

        def bmid(ap, n):
            return ap.unsqueeze(1).to_broadcast([ap.shape[0], n, ap.shape[1]])

        pool_step, dve_step, act_step = sem("pool_step"), sem("dve_step"), sem("act_step")
        consts_ready = sem("consts_ready")
        vecs_in, smalls_in = sem("vecs_in"), sem("smalls_in")
        x_in = [sem(f"x_in{i}") for i in range(3)]
        slab_in = [sem(f"slab_in{i}") for i in range(RING)]
        brow_in = [sem("brow_in0"), sem("brow_in1")]
        vcol_full, vcol_done, scol_done = sem("vcol_full"), sem("vcol_done"), sem("scol_done")
        mod_full, mrow_full, modT_full, modT_done = sem("mod_full"), sem("mrow_full"), sem("modT_full"), sem("modT_done")
        gs_done = sem("gs_done")
        sumsq_done, msq_done, rstd_done = sem("sumsq_done"), sem("msq_done"), sem("rstd_done")
        SQ_M, SQ_S, SQ_N2, SQ_F = NT, NT + 1, 2 * NT + 1, 3 * NT + 1
        RS_M, RS_S, RS_N2, RS_F = 1, 2, 3, NT + 3
        xn_done, xt_full, xt_act, xt_dve = sem("xn_done"), sem("xt_full"), sem("xt_act"), sem("xt_dve")
        pj_full, pj_act, pj_dve = sem("pj_full"), sem("pj_act"), sem("pj_dve")
        conv_mid, conv_sum, conv_done = sem("conv_mid"), sem("conv_sum"), sem("conv_done")
        spill_in = [sem(f"spill_in{i}") for i in range(4)]
        state_in, out_done = sem("state_in"), sem("out_done")
        gm_full, gm_dve, gm_act = sem("gm_full"), sem("gm_dve"), sem("gm_act")
        mD, mL, mE, mS, mP, mN, mJ, mU, mW, mC, mH = (sem(n) for n in (
            "m_rows_full", "m_log_done", "m_exp_done", "m_scores_full", "m_weights_done", "m_intra_full", "m_inter_full",
            "m_update_full", "m_wkv_done", "m_state_done", "m_num_done"))
        m_post_h, m_rows_full, m_rows_act, m_rows_dve = (sem(n) for n in (
            "m_post_h", "m_out_full", "m_out_act", "m_out_dve"))
        sD, sL, sE, sS, sP, sN, sJ, sT, sU, sX, sW, sHT, sH, sY = (sem(n) for n in (
            "s_rows_full", "s_log_done", "s_exp_done", "s_scores_full", "s_weights_done", "s_intra_full", "s_inter_full",
            "s_inter_done", "s_update_full", "s_xdt_done", "s_wkx_done", "s_decayed", "s_state_done", "s_y_done"))
        y_init, z_in, s_y, s_rows_f, s_rows_a, s_rows_d = (sem(n) for n in (
            "s_y_init", "z_in", "s_post_y", "s_out_full", "s_out_act", "s_out_dve"))
        yz = sem("s_post_gated")
        tab_in = [sem("table_in0"), sem("table_in1")]
        tab_done, cache_in = sem("table_done"), sem("cache_in")
        aS, aX, aM, aE, aR, aT, aPa, aPd, aO, aN = (sem(n) for n in (
            "a_scores_full", "a_biased", "a_max_done", "a_exp_done", "a_probs_ready", "a_turned_full", "a_turned_act",
            "a_turned_dve",
            "a_out_full", "a_out_done"))
        wo_full, wo_mul, x1_done, xt_in = sem("wo_full"), sem("wo_mul"), sem("x1_done"), [sem("xt_in0"), sem("xt_in1")]
        n2_done, n2_out = sem("n2_rows"), [sem("n2_rows_out0"), sem("n2_rows_out1")]
        h2_full, h2_act, h2_dve, rw_in, r_full = (sem(n) for n in ("h2_full", "h2_act", "h2_dve", "router_in", "logits_full"))
        r_sub, r_exp, r_aff, affT_full, k_done, kT_full, k_cols = (sem(n) for n in (
            "r_sub", "r_exp", "affinity_done", "affinityT_full", "topk_done", "topk_turned", "topk_columns"))
        zero_done, acc_zero = sem("zero_done"), sem("acc_zeroed")
        w_in_slot = [sem(f"w_slot{i}_in") for i in range(6)]
        e_h1, e_h3, e_sil, e_hid = sem("e_h1_full"), sem("e_h3_full"), sem("e_silu_done"), sem("e_hidden_done")
        xgl_in, xgc_in, ex_full, ex_act, ex_dve = (sem(n) for n in (
            "e_gather_latent", "e_gather_context", "e_x_full", "e_x_act", "e_x_dve"))
        e_yt, e_yA, e_yD, e_ty, e_yeA, e_yeD, e_free = (sem(n) for n in (
            "e_yT_full", "e_yT_act", "e_yT_dve", "e_y_turned", "e_y_act", "e_y_dve", "e_y_free"))
        sc_l, sc_c = sem("e_scatter_latent"), sem("e_scatter_context")
        gcur_set, idx_set, xc_mid = sem("e_gate_set"), sem("e_index_set"), sem("e_xc_scaled")
        fg_in = sem("fg_in")
        f_mul, f_x2, f_y = sem("f_mul"), sem("f_x2"), sem("f_y")
        y_out = sem("y_out")
        m_h_done, mo_in = sem("m_h_done"), sem("mo_in")

        last_read = {}
        for m, s in enumerate(list(range(8)) + list(range(G1, G1 + 16))):
            last_read[s] = (mod_full, m + 1)
        for j in range(4):
            last_read[WOUT + j] = (wo_full, NT)
        for n, g in enumerate(groups):
            if g[0] in "TR":
                last_read[g[1]] = (pj_full, pe_index[n] + 1)

        def pj_bank(q):
            return bk[4 + q % 4] if q < pe_index[n_first] else bk[3]

        block = ctx.enter_context(nc.Block())

        UNITS = []
        for step in range(NT):
            UNITS.append((0, step))
            UNITS.append((1, 0 if step == 0 else NT - step))
        NU = len(UNITS)

        def first_visit(u):
            d, ch = UNITS[u]
            return UNITS.index((1 - d, ch)) > u

        def state_of(u):
            d, ch = UNITS[u]
            return (0 if ch == 0 else 2) + d

        gates = [8, 9, 10, 11, 20, 21, 22, 23]

        AU = [(h, j) for h in range(HN) for j in range(-1, NL)]

        def key_tile(j):
            return min(max(j - 2, 0), 4)

        def n_local(j):
            return 0 if j < 0 else (9 * GRID if 2 <= j <= 5 else 8 * GRID)

        def turned(a):
            return sum(1 for _, j in AU[:a + 1] if j >= 0)

        @block.sync
        def _(sp):
            for dst, src, rows in ((V_C, c_ctx, 8), (V_C + 8, c, 8), (V_ADAB, ada_b, 48), (V_N1, norm1_g, 8),
                                   (V_N2, norm2_g, 8), (V_MG, m_norm_g, 2), (V_SG, s_norm_g, 3), (V_CB, conv_b, 5),
                                   (V_CW, conv_w, 15)):
                sp.dma_start(vecs[dst:dst + rows, :], src.rearrange("(a b) -> a b", b=P)).then_inc(vecs_in, 16)
            for dst, src, n in ((R_FB, f_bias, 8), (R_DTB, dt_bias, 12), (R_ALOG, a_log, 12), (R_D, d_skip, 6),
                                (R_M0, state_m, 8)):
                sp.dma_start(smalls[:, dst:dst + n], src.rearrange("(a b) -> a b", a=1)).then_inc(smalls_in, 16)

            def load_slab(s):
                mat, a, n = slabs[s]
                if s >= RING:
                    sp.wait_ge(*last_read[s - RING])
                sp.dma_start(ring[:, s % RING, :, 0:n], w_src[mat][:, :, a:a + n]).then_inc(slab_in[s % RING], 16)

            sp.dma_start(X[:, 0, :], x_prompt).then_inc(x_in[0], 16)
            for s in range(RING):
                load_slab(s)
                for i in (2 * s + 1, 2 * s + 2):
                    sp.dma_start(X[:, i, :], x_sample[(i - 1) * P:i * P, :]).then_inc(x_in[i // 3], 16)
            sp.wait_ge(consts_ready, 1)
            for d in range(NDIR):
                for h in range(HM):
                    dst = Cst[HD * (h % 2):HD * (h % 2) + HD, 2 + d, h % 2, h // 2, :]
                    sp.dma_start(dst[:, 0:HD], state_c[d, h]).then_inc(state_in, 16)
                    sp.dma_start(dst[:, HD:HD + 1], state_n[d, h].rearrange("(a b) -> a b", b=1)).then_inc(state_in, 16)
                for g in range(GS):
                    half_g = slice(HD * g, HD * g + HD)
                    sp.dma_start(Hst[half_g, 2 + d, g, :], state_sT[d, half_g, :]).then_inc(state_in, 16)
            for s in range(RING, G1):
                load_slab(s)
            sp.wait_ge(pj_full, len(pe_groups))
            for h in range(HN):
                if h >= 2:
                    sp.wait_ge(aX, 9 * (h - 1))
                for o in (0, 1):
                    first = rpb_pad[64 + (h * 15 + 1 - o) * 31 + 15 - (GRID - 1):][0:1]
                    src = bass.AP(tensor=first.tensor, offset=first.offset, ap=[[1, GRID], [31, 14], [1, GRID]])
                    sp.dma_start(tb[GRID * o:GRID * o + GRID, h % 2], src).then_inc(tab_in[h % 2], 16)

            for m in range(8, 24):
                load_slab(G1 + m - 8)
                if m in gates:
                    i = gates.index(m)
                    if i >= 2:
                        sp.wait_ge(modT_full, gates[i - 2] + 1)
                    sp.dma_start(brow[:, i % 2, :], ada_b[m * SLAB:m * SLAB + SLAB].rearrange("(a b) -> a b", a=1))\
                        .then_inc(brow_in[i % 2], 16)
            for j in range(4):
                load_slab(WOUT + j)
            sp.wait_ge(aO, len(AU))
            sp.dma_start(rw, router_w.rearrange("(k p) e -> p k e", p=P)).then_inc(rw_in, 16)
            for i in range(NT):
                if i >= 2:
                    sp.wait_ge(x1_done, i - 1)
                src = x_prompt if i == 0 else x_sample[(i - 1) * P:i * P, :]
                sp.dma_start(xt[:, i % 2, :], src).then_inc(xt_in[i % 2], 16)

            w13 = [w.rearrange("e (k p) f -> e p k f", p=P) for w in (exp_w1, exp_w3)]
            w2v = exp_w2.rearrange("e (k p) d -> e p k d", p=P)

            def expert_slab(e, q):
                half_q, src = (q // 2, w13[q % 2]) if q < 4 else (q - 4, w2v)
                one = src[e:e + 1] if isinstance(e, int) else src[bass.ds(e, 1)]
                one = one.rearrange("e p k f -> (e p) k f")
                sp.dma_start(wslot[q], one[:, :, 512 * half_q:512 * half_q + 512]).then_inc(w_in_slot[q], 16)

            sp.wait_ge(wo_full, NT)
            for q in (0, 1, 4, 5):
                expert_slab(0, q)
            sp.wait_ge(wo_mul, NT)
            sp.wait_ge(x1_done, NT)
            sp.wait_ge(r_full, NT)
            sp.wait_ge(n2_out[0], 16 * 5)
            sp.wait_ge(n2_out[1], 16 * 4)
            for q in (2, 3):
                expert_slab(0, q)
            with sp.Fori(1, NE) as e:
                for q in range(6):
                    if q < 4:
                        sp.wait_ge(e_h3 if q % 2 else e_h1, e * KD + (KD // 2 * (q // 2 + 1) - KD))
                    else:
                        sp.wait_ge(e_yt, e * KD + (KD // 2 * (q - 3) - KD))
                    expert_slab(e, q)

            sp.wait_ge(e_yt, KD * NE)
            sp.dma_start(fgb, bass.AP(tensor=final_g.tensor, offset=final_g.offset, ap=[[0, P], [1, D]])).then_inc(fg_in, 16)
            sp.wait_ge(e_free, NE + 1)
            for i in range(NT):
                src = accc_d if i == 0 else accl_d[(i - 1) * P:i * P, :]
                sp.dma_start(y9[:, i, :], src).then_inc(x_in[i // 3], 16)
            for i in range(NT):
                sp.wait_ge(f_y, i + 1)
                dst = y_prompt if i == 0 else y_sample[(i - 1) * P:i * P, :]
                sp.dma_start(dst, y9[:, i, :]).then_inc(y_out, 16)
            sp.wait_ge(y_out, 16 * NT)
            sp.wait_ge(out_done, 16 * 24)

        @block.gpsimd
        def _(pool):
            steps = [0]

            def link(ins):
                steps[0] += 1
                ins.then_inc(pool_step, 1)
                pool.wait_ge(pool_step, steps[0])

            pool.memset(ident[:], 0.0)
            pool.memset(upto[:], 1.0)
            pool.memset(downto[:], 1.0)
            pool.memset(mask[0][:], 0.0)
            link(pool.memset(mask[1][:], 0.0))
            pool.affine_select(out=ident[:], in_=ident[:], compare_op=ALU.not_equal, fill=1.0, base=0,
                               pattern=[[-1, P]], channel_multiplier=1)
            for t, m, fill in ((upto, mask[0], 0.0), (downto, mask[1], 0.0)):
                sign = 1 if t is upto else -1
                for dst, f in ((t, 0.0), (m, NEG)):
                    pool.affine_select(out=dst[:], in_=dst[:], compare_op=ALU.is_ge, fill=f, base=0,
                                       pattern=[[sign, P]], channel_multiplier=-sign)
            pool.memset(half[:], -0.5)
            pool.memset(gt[:], 0.0)
            pool.memset(Cst[:], 0.0)
            pool.memset(Hst[:], 0.0)
            pool.memset(ones[:], 1.0)
            pool.memset(small[:], 0.0).then_inc(consts_ready, 1)

            pool.wait_ge(msq_done, 1)
            pool.tensor_tensor(rstd[:, 0, :], rstd[:, 0, :], half[:, 0:NT], ALU.pow).then_inc(rstd_done, 1)

            pool.wait_ge(xt_act, NT)
            pool.wait_ge(xt_dve, NT)
            pool.memset(v1[:, :, :, HD:HD + 1], 1.0)
            for col in (0, P + 1, P + 2, T + 3):
                pool.memset(raw[:, :, col:col + 1], 0.0).then_inc(consts_ready, 1)

            pool.wait_ge(gm_act, 4)
            pool.wait_ge(pj_dve, evacuated("D", n_first))
            pool.wait_ge(conv_done, 5)
            for u, (d, ch) in enumerate(UNITS):
                if u >= 2:
                    pool.wait_ge(mU, u - 1)
                pool.tensor_tensor(wkv[:, u % 2], v1[:, ch], bc(gate(WKM, d)[:, ch, :], HD + 1), ALU.mult)\
                    .then_inc(mW, 1)

            pool.wait_ge(msq_done, RS_M + 1)
            pool.tensor_tensor(small[:, 0, 0:36], small[:, 0, 0:36], half[:, 0:36], ALU.pow).then_inc(rstd_done, 1)

            pool.wait_ge(m_post_h, 1)
            pool.wait_ge(m_rows_full, NT)
            for i in range(NT):
                pool.tensor_tensor(yacc[:, i].rearrange("p (h v) -> p h v", v=HD),
                                   xrows[:, i].rearrange("p (h v) -> p h v", v=HD),
                                   bc(smb[:, R_D:R_D + HS], HD), ALU.mult).then_inc(y_init, 1)
            for u, (d, ch) in enumerate(UNITS):
                if u >= 1:
                    pool.wait_ge(sHT, u)
                x3 = xrows[:, ch].rearrange("p (h v) -> p h v", v=HD)
                if u >= 2:
                    pool.wait_ge(sN, u - 1)
                pool.tensor_tensor(xdt[:, u % 2], x3, bc(gate(DT, d, HS)[:, ch, :], HD), ALU.mult).then_inc(sX, 1)
                if u >= 2:
                    pool.wait_ge(sU, u - 1)
                pool.tensor_tensor(wkx[:, u % 2], x3, bc(gate(SWK, d, HS)[:, ch, :], HD), ALU.mult).then_inc(sW, 1)
                if u >= 1:
                    pool.wait_ge(sH, u)
                pool.wait_ge(sW, u + 1)
                for g in range(GS):
                    q = slice(HD * g, HD * g + HD)
                    if g:
                        link(ins)
                    ins = pool.tensor_tensor(hs[q, :].rearrange("p (r v) -> p r v", v=HD),
                                             Hst[q, state_of(u), g, :].rearrange("p (r v) -> p r v", v=HD),
                                             bc(gate(SEL, d, HS)[q, ch, RS * g:RS * g + RS], HD), ALU.mult)
                ins.then_inc(sHT, 1)
            pool.wait_ge(sY, NU)
            pool.memset(zero, 0.0).then_inc(zero_done, 1)
            pool.wait_ge(msq_done, RS_S + 1)
            pool.tensor_tensor(rstd[:, 1, :], rstd[:, 1, :], half[:, 0:NT], ALU.pow).then_inc(rstd_done, 1)

            for h in range(HN):
                t = tb[:, h % 2]
                pool.wait_ge(tab_in[h % 2], 32 * (h // 2 + 1))
                for o in (0, GRID):
                    a, b = t[o:o + GRID, :, 0:48], t[o:o + GRID, :, 16:GRID]
                    link(pool.affine_select(out=a, in_=a, compare_op=ALU.is_ge, fill=NEG, base=7 - 63,
                                            pattern=[[0, 14], [1, 48]], channel_multiplier=1))
                    link(pool.affine_select(out=b, in_=b, compare_op=ALU.is_ge, fill=NEG, base=8 + 47,
                                            pattern=[[0, 14], [-1, 48]], channel_multiplier=-1))
                if h >= 2:
                    pool.wait_ge(aX, 9 * (h - 1))
                link(pool.tensor_copy(ti[:, h % 2], t[:, 2:11, :]))
                link(pool.memset(ti[0:GRID, h % 2, 8, :], NEG))
                pool.memset(ti[GRID:P, h % 2, 0, :], NEG).then_inc(tab_done, 1)
                pool.wait_ge(tab_done, h + 1)

            for i in range(NT):
                pool.wait_ge(wo_mul, i + 1)
                pool.wait_ge(xt_in[i % 2], 16 * (i // 2 + 1))
                pool.tensor_tensor(x1[:, i, :], xt[:, i % 2, :], tw[:, i % 2, :], ALU.add).then_inc(x1_done, 1)
                pool.wait_ge(msq_done, RS_N2 + i + 1)
                pool.tensor_tensor(rstd[:, 2, i:i + 1], rstd[:, 2, i:i + 1], half[:, 0:1], ALU.pow).then_inc(rstd_done, 1)

            pool.wait_ge(k_cols, 1)
            pool.wait_ge(n2_out[0], 16 * 5)
            pool.wait_ge(n2_out[1], 16 * 4)
            pool.wait_ge(acc_zero, 16 * NT)
            pool.indirect_dma_start(out=xg, out_offset=None, in_=h2l_d, in_offset=bass.IndirectOffsetOnAxis(
                ap=icur[:, 0:1].bitcast(U32), axis=0)).then_inc(xgl_in, 16)
            pool.indirect_dma_start(out=xgc[0:CAPC, :], out_offset=None, in_=h2c_d, in_offset=bass.IndirectOffsetOnAxis(
                ap=icur[0:CAPC, 1:2].bitcast(U32), axis=0)).then_inc(xgc_in, 16)
            pool.sem_inc(e_free, 1)
            with pool.Fori(0, NE) as e:
                pool.wait_ge(ex_full, e + 1)
                pool.wait_ge(xgl_in, (e + 1) * 16)
                pool.wait_ge(xgc_in, (e + 1) * 16)
                pool.tensor_copy(icur[:, 0:1], il[:, bass.ds(e + 1, 1)]).then_inc(idx_set, 1)
                pool.wait_ge(idx_set, e * 6 + 1)
                pool.tensor_copy(icur[0:CAPC, 1:2], ic[0:CAPC, bass.ds(e + 1, 1)]).then_inc(idx_set, 1)
                pool.wait_ge(idx_set, e * 6 + 2)
                pool.sem_inc(idx_set, 1)
                pool.indirect_dma_start(out=xg, out_offset=None, in_=h2l_d, in_offset=bass.IndirectOffsetOnAxis(
                    ap=icur[:, 0:1].bitcast(U32), axis=0)).then_inc(xgl_in, 16)
                pool.indirect_dma_start(out=xgc[0:CAPC, :], out_offset=None, in_=h2c_d, in_offset=bass.IndirectOffsetOnAxis(
                    ap=icur[0:CAPC, 1:2].bitcast(U32), axis=0)).then_inc(xgc_in, 16)
                pool.tensor_copy(icur[:, 2:3], il[:, bass.ds(e, 1)]).then_inc(idx_set, 1)
                pool.wait_ge(idx_set, e * 6 + 4)
                pool.tensor_copy(icur[0:CAPC, 3:4], ic[0:CAPC, bass.ds(e, 1)]).then_inc(idx_set, 1)
                pool.wait_ge(idx_set, e * 6 + 5)
                pool.wait_ge(e_yeA, e + 2)
                pool.wait_ge(e_yeD, e + 2)
                pool.sem_inc(idx_set, 1)
                pool.indirect_dma_start(out=accl_d, out_offset=bass.IndirectOffsetOnAxis(
                    ap=icur[:, 2:3].bitcast(U32), axis=0), in_=ye, in_offset=None, compute_op=ALU.add).then_inc(sc_l, 16)
                pool.indirect_dma_start(out=accc_d, out_offset=bass.IndirectOffsetOnAxis(
                    ap=icur[0:CAPC, 3:4].bitcast(U32), axis=0), in_=yec[0:CAPC, :], in_offset=None,
                    compute_op=ALU.add).then_inc(sc_c, 16)
                pool.wait_ge(sc_l, (e + 1) * 16)
                pool.wait_ge(sc_c, (e + 1) * 16)
                pool.sem_inc(e_free, 1)
            pool.wait_ge(xgl_in, 16 * (NE + 1))
            pool.wait_ge(xgc_in, 16 * (NE + 1))

            for i in range(NT + 2):
                if i < NT:
                    pool.wait_ge(f_mul, i + 1)
                    pool.tensor_tensor(y9[:, i, :], y9[:, i, :], x1[:, i, :], ALU.add).then_inc(f_x2, 1)
                if i >= 2:
                    q = i - 2
                    pool.wait_ge(msq_done, RS_F + q + 1)
                    pool.tensor_tensor(rstd[:, 3, q:q + 1], rstd[:, 3, q:q + 1], half[:, 0:1], ALU.pow).then_inc(rstd_done, 1)

        @block.scalar
        def _(act):
            steps = [0]

            def link(ins):
                steps[0] += 1
                ins.then_inc(act_step, 1)
                act.wait_ge(act_step, steps[0])

            def mod_row(m):
                act.wait_ge(mod_full, m + 1)
                if m >= 2:
                    act.wait_ge(modT_full, m - 1)
                nc.scalar.activation(mrow[0:2, m % 2, :], bk[1 + m % 2][0:2, 0:SLAB], ACT.Copy).then_inc(mrow_full, 1)

            act.wait_ge(vcol_done, 1)
            nc.scalar.activation(scol[:], vcol[:, V_C:V_C + 16], ACT.Silu).then_inc(scol_done, 1)
            for i in range(NT):
                act.wait_ge(x_in[i // 3], 48)
                if i >= 2:
                    act.wait_ge(sumsq_done, i - 1)
                nc.scalar.activation(sq_junk[:, i % 2, :], X[:, i, :], ACT.Square,
                                     accum_out=sumsq[:, 0, i:i + 1]).then_inc(sumsq_done, 1)
                for m in {2: (0, 1), 5: (2,), 8: (3, 4, 5, 6, 7)}.get(i, ()):
                    mod_row(m)
            act.wait_ge(gs_done, 1)
            for i in range(NT):
                act.wait_ge(xt_full, i + 1)
                s = min(i, 1)
                for k in range(4):
                    ins = nc.scalar.activation(hT[:, k, i * P:i * P + P], bk[4 + 2 * (i % 2)][:, k * P:k * P + P],
                                               ACT.Identity, scale=gs[0][:, k, s:s + 1], bias=modcol[:, k, s:s + 1])
                ins.then_inc(xt_act, 1)

            act.wait_ge(consts_ready, 5)
            spills = [0]

            def spill(func, dst, src, n):
                slot, use = spills[0] % 4, spills[0] // 4
                spills[0] += 1
                if use:
                    act.wait_ge(spill_in[slot], 16 * use)
                link(nc.scalar.activation(stage[:, slot, 0:n], src, func))
                act.dma_start(dst, stage[:, slot, 0:n]).then_inc(spill_in[slot], 16)

            def evacuate(n):
                kind, _, _, cols, i, target, engine = groups[n]
                if kind == "C":
                    conv(target[1])
                    return
                if engine != "A":
                    return
                q = pe_index[n]
                act.wait_ge(pj_full, q + 1)
                ps = pj_bank(q)
                tok = slice(i * P, i * P + P)
                if kind == "T":
                    dst, sc = {"qT": (qT, 1.0), "kT": (kT, SCALE), "nqT": (nqT, SCALE), "nkT": (nkT, 1.0)}[target[0]]
                    ins = nc.scalar.activation(dst[:, target[1], i * 384:i * 384 + 384], ps[:, 0:384], ACT.Copy, scale=sc)
                elif kind == "X":
                    (_, b), (where, _) = target
                    dst = krows if where == "krows" else (xrows if b < 3 else brows)
                    col = b * P if (where == "krows" or b < 3) else 0
                    ins = nc.scalar.activation(dst[:, 3 * i:3 * i + 3, col:col + P],
                                               ps[:, 0:384].rearrange("p (a b) -> p a b", b=P), ACT.Copy)
                elif target[0] == "mo":
                    spill(ACT.Sigmoid, mo_d[tok, :], ps[:, 0:256], 256)
                    act.sem_inc(pj_act, 1)
                    return
                elif target[0] == "gz":
                    spill(ACT.Silu, z_d[tok, 0:240], ps[:, 16:256], 240)
                    ins = nc.scalar.activation(G[:, i, :], ps[:, 0:16], ACT.Copy)
                elif target[0] == "z2":
                    spill(ACT.Silu, z_d[tok, 240:384], ps[:, 0:144], 144)
                    act.sem_inc(pj_act, 1)
                    return
                elif target[0] == "nv":
                    ins = nc.scalar.activation(nv[:, i, target[1]:target[1] + cols], ps[:, 0:cols], ACT.Copy)
                ins.then_inc(pj_act, 1)

            def conv(b):
                w = raw[:, b % 2, :]
                act.wait_ge(pj_dve, evacuated("D", last_of(("raw", b)) + 1))
                if b in (2,):
                    act.wait_ge(pj_full, pe_index[last_of((("conv", 0), ("xrows", 0)))] + 1)
                out = conv_out(b)
                nc.scalar.activation(out, w[:, 1:T + 3], ACT.Identity, scale=vcol[:, V_CW + 5 + b:V_CW + 6 + b],
                                     bias=vcol[:, V_CB + b:V_CB + b + 1]).then_inc(conv_mid, 1)
                act.wait_ge(conv_sum, b + 1)
                nc.scalar.activation(out, out, ACT.Silu).then_inc(conv_done, 1)

            for n in range(n_first):
                evacuate(n)

            act.wait_ge(conv_sum, 5)
            for i in range(4):
                act.wait_ge(spill_in[i], 16 * ((27 - i + 3) // 4))
            act.dma_start(mo, mo_d.rearrange("(t p) n -> p t n", p=P)).then_inc(mo_in, 16)
            act.wait_ge(gm_dve, 1)
            nc.scalar.activation(gate(FE), gate(FL), ACT.Abs)
            link(nc.scalar.activation(gate(DTE), gate(DT), ACT.Abs))
            nc.scalar.activation(gate(FE), gate(FE), ACT.Exp, scale=-1.0)
            nc.scalar.activation(smb[:, R_ALOG:R_ALOG + 12], smb[:, R_ALOG:R_ALOG + 12], ACT.Exp).then_inc(gm_act, 1)
            link(nc.scalar.activation(gate(DTE), gate(DTE), ACT.Exp, scale=-1.0))
            nc.scalar.activation(gate(FE), gate(FE), ACT.Ln, bias=1.0).then_inc(gm_act, 1)
            nc.scalar.activation(gate(DTE), gate(DTE), ACT.Ln, bias=1.0).then_inc(gm_act, 1)
            act.wait_ge(gm_dve, 9)
            for t in (WINT, EMT, WKM, DEC, SEA, SWK, SEL):
                ins = nc.scalar.activation(gate(t), gate(t), ACT.Exp)
            ins.then_inc(gm_act, 1)

            for u in range(NU):
                act.wait_ge(mL, u + 1)
                nc.scalar.activation(Lm[:, u % 2], Lm[:, u % 2], ACT.Exp).then_inc(mE, 1)

            act.wait_ge(mC, 2)
            for d in range(NDIR):
                for h in range(HM):
                    src = Cst[HD * (h % 2):HD * (h % 2) + HD, d, h % 2, h // 2, :]
                    act.dma_start(new_c[d, h], src[:, 0:HD]).then_inc(out_done, 16)
                    act.dma_start(new_n[d, h].rearrange("(a b) -> a b", b=1), src[:, HD:HD + 1]).then_inc(out_done, 16)
                act.dma_start(new_m[d].rearrange("(a b) -> a b", a=1),
                             gate(MN, d)[0:1, 0, :]).then_inc(out_done, 16)

            act.wait_ge(m_h_done, NU)
            nc.scalar.activation(SQ, hacc, ACT.Square).then_inc(sumsq_done, 1)
            for i in range(NT):
                if i % 2 == 0:
                    act.wait_ge(m_rows_full, i + 1)
                    for b in range(2):
                        ins = nc.scalar.activation(mixM[:, b, i * P:i * P + P], bk[4 + i % 2][:, b * P:b * P + P], ACT.Copy,
                                                   scale=vcol[:, V_MG + b:V_MG + b + 1])
                    ins.then_inc(m_rows_act, 1)

            second = iter(range(n_first, len(groups)))
            act.wait_ge(m_rows_full, NT)
            for u in range(NU):
                for g in range(GS):
                    act.wait_ge(sL, 2 * u + g + 1)
                    nc.scalar.activation(Ls[:, u % 2, g], Ls[:, u % 2, g], ACT.Exp).then_inc(sE, 1)
                    evacuate(next(second))
            act.wait_ge(sH, 2)
            for d in range(NDIR):
                for g in range(GS):
                    q = slice(HD * g, HD * g + HD)
                    act.dma_start(new_sT[d, q, :], Hst[q, d, g, :]).then_inc(out_done, 16)
            act.dma_start(new_kT.rearrange("(b p) t -> p b t", p=P), nkT[:, :, 0:P]).then_inc(out_done, 16)
            act.dma_start(new_v, nv[:, 0, :]).then_inc(out_done, 16)
            act.wait_ge(sY, NU)
            act.wait_ge(sU, NU)
            act.dma_start(z, z_d.rearrange("(t p) n -> p t n", p=P)).then_inc(z_in, 16)
            act.wait_ge(pj_full, len(pe_groups))
            act.dma_start(ckT, cacheT_k.rearrange("(b p) t -> p b t", p=P)).then_inc(cache_in, 16)
            act.dma_start(cv, cache_v).then_inc(cache_in, 16)
            act.wait_ge(zero_done, 1)
            for i in range(NT):
                act.dma_start(accc_d if i == 0 else accl_d[(i - 1) * P:i * P, :], zero).then_inc(acc_zero, 16)
            act.wait_ge(yz, 1)
            for i in range(NT):
                if i >= 2:
                    act.wait_ge(sumsq_done, SQ_S + i - 1)
                nc.scalar.activation(sc_sb[:, i % 2, 0:384], yacc[:, i], ACT.Square, accum_out=sumsq[:, 1, i:i + 1])\
                    .then_inc(sumsq_done, 1)
            for i in range(0, NT, 2):
                act.wait_ge(s_rows_f, i + 1)
                for b in range(3):
                    ins = nc.scalar.activation(mixS[:, b, i * P:i * P + P], bk[4 + i % 2][:, b * P:b * P + P], ACT.Copy,
                                               scale=vcol[:, V_SG + b:V_SG + b + 1])
                ins.then_inc(s_rows_a, 1)

            def a_exp(a):
                _, j = AU[a]
                n = n_local(j) + P
                act.wait_ge(aM, a + 1)
                nc.scalar.activation(sc_sb[:, a % 2, 0:n], sc_sb[:, a % 2, 0:n], ACT.Exp, bias=nmax[:, a:a + 1],
                                     accum_out=ssum[:, a:a + 1]).then_inc(aE, 1)

            def a_turn(a):
                if AU[a][1] < 0:
                    return
                act.wait_ge(aT, a + 1)
                if a >= 2:
                    act.wait_ge(aO, a - 1)
                nc.scalar.activation(pT[:, a % 2, 0:4, :], bk[4].rearrange("p (m q) -> p m q", q=P), ACT.Copy)\
                    .then_inc(aPa, 1)

            act.wait_ge(msq_done, RS_S + 1)
            a_exp(0)
            for a in range(len(AU)):
                if a + 1 < len(AU):
                    a_exp(a + 1)
                a_turn(a)

            for m in range(8, 24):
                mod_row(m)
            act.wait_ge(gs_done, 2)
            for i in range(NT + 1):
                if i >= 1:
                    q = i - 1
                    act.wait_ge(h2_full, q + 1)
                    if q >= 2:
                        act.wait_ge(r_full, q - 1)
                    s = min(q, 1)
                    for k in range(4):
                        ins = nc.scalar.activation(h2T[:, q % 2, k * P:k * P + P], bk[1][:, k * P:k * P + P],
                                                   ACT.Identity, scale=gs[1][:, k, s:s + 1],
                                                   bias=modcol[:, 24 + k, s:s + 1])
                    ins.then_inc(h2_act, 1)
                if i < NT:
                    act.wait_ge(x1_done, i + 1)
                    act.wait_ge(sumsq_done, SQ_N2 + i)
                    nc.scalar.activation(sq2, x1[:, i, :], ACT.Square, accum_out=sumsq[:, 2, i:i + 1])\
                        .then_inc(sumsq_done, 1)
                    act.wait_ge(n2_done, i + 1)
                    act.dma_start(h2c_d if i == 0 else h2l_d[(i - 1) * P:i * P, :], nrow[:, i % 2, :])\
                        .then_inc(n2_out[i % 2], 16)
            act.wait_ge(r_sub, 1)
            nc.scalar.activation(aff, lg, ACT.Exp).then_inc(r_exp, 1)

            def x_evac():
                for k in range(4):
                    ins = nc.scalar.activation(xeT[:, k, 0:P], bk[6][:, k * P:k * P + P], ACT.Identity,
                                               scale=gs[1][:, k, 1:2], bias=modcol[:, 24 + k, 1:2])
                ins.then_inc(ex_act, 1)

            act.wait_ge(ex_full, 1)
            x_evac()
            act.sem_inc(e_yA, 1)
            act.sem_inc(e_yeA, 1)
            with act.Fori(0, NE) as e:
                for fb in range(KD):
                    act.wait_ge(e_h1, e * KD + (fb + 1))
                    act.wait_ge(e_hid, e * KD + (fb + 1))
                    nc.scalar.activation(sil[:, fb % 2, :], bk[fb % 2][:, 0:SLOTS], ACT.Silu).then_inc(e_sil, 1)
                act.wait_ge(ex_full, e + 2)
                x_evac()
                for db in range(0, KD, 2):
                    act.wait_ge(e_yt, e * KD + (db + 1))
                    nc.scalar.activation(yT[:, db, :], bk[4][:, 0:SLOTS], ACT.Copy).then_inc(e_yA, 1)
                act.wait_ge(e_ty, e + 1)
                act.wait_ge(e_free, e + 1)
                act.wait_ge(gcur_set, e + 1)
                nc.scalar.activation(ye[:, 0:512], bk[6], ACT.Copy, scale=gcur[:, 0:1]).then_inc(e_yeA, 1)

            for i in range(NT):
                act.wait_ge(f_x2, i + 1)
                if i >= 2:
                    act.wait_ge(sumsq_done, SQ_F + i - 1)
                nc.scalar.activation(sq3[:, i % 2, :], y9[:, i, :], ACT.Square, accum_out=sumsq[:, 3, i:i + 1])\
                    .then_inc(sumsq_done, 1)

        @block.tensor
        def _(pe):
            mm = nc.tensor.matmul

            def slab_ready(s):
                pe.wait_ge(slab_in[s % RING], 16 * (s // RING + 1))

            def mods(ms, slab0):
                prev = None
                for m in list(ms) + [None]:
                    if m is not None:
                        s = slab0 + m - ms[0]
                        slab_ready(s)
                        if m >= 2:
                            pe.wait_ge(mrow_full, m - 1)
                        for k in range(KD):
                            ins = mm(bk[1 + m % 2][0:2, 0:SLAB], scol[:, k:k + 9:8], ring[:, s % RING, k, :],
                                     start=(k == 0), stop=(k == KD - 1))
                        ins.then_inc(mod_full, 1)
                    if prev is not None:
                        pe.wait_ge(mrow_full, prev + 1)
                        if prev >= 1:
                            pe.wait_ge(modT_done, prev)
                        if prev in gates:
                            i = gates.index(prev)
                            pe.wait_ge(brow_in[i % 2], 16 * (i // 2 + 1))
                            for j in range(2):
                                mm(bk[3][:, j * SLAB:j * SLAB + SLAB], ident[0:2, j:j + 1].to_broadcast([2, P]),
                                   mrow[0:2, prev % 2, :], start=True, stop=False)
                                ins = mm(bk[3][:, j * SLAB:j * SLAB + SLAB], ones[0:1, :], brow[0:1, i % 2, :],
                                         start=False, stop=True)
                        for b in range(0 if prev in gates else 2):
                            ins = nc.tensor.transpose(bk[3][:, 2 * b:2 * b + 2], mrow[0:2, prev % 2, b * P:b * P + P],
                                                      ident[0:2, 0:2])
                        ins.then_inc(modT_full, 1)
                    prev = m

            pe.wait_ge(consts_ready, 1)
            pe.wait_ge(vecs_in, 16 * 9)
            nc.tensor.transpose(bk[0][:, 0:V_END], vecs[0:V_END, :], ident[0:V_END, 0:V_END])
            pe.wait_ge(smalls_in, 16 * 5)
            mm(bk[0][:, 128:128 + R_END], ones[0:1, :], smalls[0:1, :], start=True, stop=True).then_inc(vcol_full, 1)
            pe.wait_ge(scol_done, 1)
            mods(range(8), 0)
            for i in range(NT):
                pe.wait_ge(xn_done, i + 1)
                if i >= 2:
                    pe.wait_ge(xt_act, i - 1)
                    pe.wait_ge(xt_dve, i - 1)
                for k in range(KD):
                    ins = nc.tensor.transpose(bk[4 + 2 * (i % 2) + k // 4][:, (k % 4) * P:(k % 4) * P + P],
                                              X[:, i, k * P:k * P + P], ident[:])
                ins.then_inc(xt_full, 1)

            def group(n):
                kind, s, col, cols, i, target, _ = groups[n]
                if kind == "C":
                    return
                q = pe_index[n]
                before = q - 4 if n < n_first else q - 1
                if before >= (0 if n < n_first else pe_index[n_first]):
                    m = [k for k, w in pe_index.items() if w == before][0]
                    if groups[m][6] == "A":
                        pe.wait_ge(pj_act, evacuated("A", m) + 1)
                    else:
                        pe.wait_ge(pj_dve, evacuated("D", m) + 1)
                ps = pj_bank(q)
                if kind == "X":
                    (src, b), (where, _) = target
                    if src in ("kT", "dtT"):
                        m = last_of((src, b)) + 1
                        pe.wait_ge(pj_act, evacuated("A", m))
                        pe.wait_ge(pj_dve, evacuated("D", m))
                    else:
                        pe.wait_ge(conv_done, b + 1)
                    for t in range(3 if src == "dtT" else 0):
                        ins = nc.tensor.transpose(ps[:, t * 2 * HS:(t + 1) * 2 * HS], dtT[0:2 * HS, (3 * i + t) * P:(3 * i + t + 1) * P],
                                                  ident[0:2 * HS, 0:2 * HS])
                    for t in range(0 if src == "dtT" else 3):
                        j = 3 * i + t
                        blk = kT[:, b, j * P:j * P + P] if src == "kT" else conv_out(b)[:, cv_tok(j):cv_tok(j) + P]
                        ins = nc.tensor.transpose(ps[:, t * P:t * P + P], blk, ident[:])
                else:
                    slab_ready(s)
                    for k in range(KD):
                        if kind == "T":
                            ins = mm(ps[0:cols, 0:384], ring[:, s % RING, k, col:col + cols], hT[:, k, i * 384:i * 384 + 384],
                                     start=(k == 0), stop=(k == KD - 1))
                        else:
                            ins = mm(ps[:, 0:cols], hT[:, k, i * P:i * P + P], ring[:, s % RING, k, col:col + cols],
                                     start=(k == 0), stop=(k == KD - 1))
                ins.then_inc(pj_full, 1)

            pe.wait_ge(xt_act, NT)
            pe.wait_ge(xt_dve, NT)
            for n in range(n_first):
                group(n)

            pe.wait_ge(vcol_done, 2)
            pe.wait_ge(gm_dve, 2)
            for bank, t, tot in ((bk[0], F, P), (bk[2], DA, P)):
                mm(bank[:, 0:GW], upto[:], gate(t)[:, 0:GW], start=True, stop=True)
                mm(bank[:, GW:2 * GW], downto[:], gate(t)[:, GW:2 * GW], start=True, stop=True)
                mm(bank[:, P:2 * P], ones[:], gate(t), start=True, stop=True).then_inc(gm_full, 1)
            pe.wait_ge(gm_dve, 3)
            nc.tensor.transpose(bk[1][:, 0:P], gate(AC), ident[:]).then_inc(gm_full, 1)
            pe.wait_ge(gm_dve, 4)
            nc.tensor.transpose(bk[3][:, 0:P], gate(SA), ident[:]).then_inc(gm_full, 1)
            pe.wait_ge(gm_dve, 5)
            nc.tensor.transpose(bk[1][:, P:2 * P], gate(CMR), ident[:]).then_inc(gm_full, 1)
            pe.wait_ge(gm_dve, 7)
            mm(bk[1][:, 256:320], ident[:, P - 1:P].to_broadcast([P, P]), gate(CMC)[:, 0:GW], start=True, stop=True)
            mm(bk[1][:, 320:384], ident[:, 0:1].to_broadcast([P, P]), gate(CMC)[:, GW:2 * GW], start=True, stop=True)\
                .then_inc(gm_full, 1)
            pe.wait_ge(gm_dve, 8)
            nc.tensor.transpose(bk[1][:, 384:512], gate(NM), ident[:]).then_inc(gm_full, 1)

            def m_rows(u):
                d, ch = UNITS[u]
                if u >= 2:
                    pe.wait_ge(mL, u - 1)
                for h in range(HM):
                    r = d * GW + ch * HM + h
                    ins = mm(bk[4 + u % 2][:, h * P:h * P + P], ident[:, r:r + 1].to_broadcast([P, P]), gate(NMR),
                             start=True, stop=True)
                ins.then_inc(mD, 1)

            def m_scores(u):
                d, ch = UNITS[u]
                if u >= 1:
                    pe.wait_ge(mP, u)
                for e in range(2):
                    q = slice(HD * e, HD * e + HD)
                    for j in range(2):
                        ins = mm(bk[6 if e == 0 else 0][:, j * P:j * P + P], kT[q, j, ch * P:ch * P + P],
                                 qT[q, j, ch * P:ch * P + P], start=True, stop=True)
                ins.then_inc(mS, 1)

            def m_state(u):
                d, ch = UNITS[u]
                if u >= 2:
                    pe.wait_ge(mC, u - 1)
                    pe.wait_ge(mH, u - 1)
                for j in range(2):
                    ins = mm(bk[2 + u % 2][:, j * 130:j * 130 + 130], qT[:, j, ch * P:ch * P + P],
                             Cst[:, state_of(u), :, j, :], start=True, stop=True)
                ins.then_inc(mJ, 1)

            def m_values(u):
                d, ch = UNITS[u]
                nu = bk[7 if u % 2 == 0 else 1]
                pe.wait_ge(mP, u + 1)
                for h in range(HM):
                    ins = mm(nu[:, h * 65:h * 65 + 65], Lm[:, u % 2, h % 2, h // 2, :], v1[:, ch, h, :],
                             start=True, stop=True)
                ins.then_inc(mN, 1)

            def m_update(u):
                d, ch = UNITS[u]
                nu = bk[7 if u % 2 == 0 else 1]
                pe.wait_ge(mW, u + 1)
                for h in range(HM):
                    q = slice(HD * (h % 2), HD * (h % 2) + HD)
                    ins = mm(nu[q, 260 + 65 * (h // 2):325 + 65 * (h // 2)], krows[:, ch, h * HD:h * HD + HD],
                             wkv[:, u % 2, h, :], start=True, stop=True)
                ins.then_inc(mU, 1)

            pe.wait_ge(gm_dve, 11)
            pe.wait_ge(pj_act, evacuated("A", n_first))
            pe.wait_ge(pj_dve, evacuated("D", n_first))
            pe.wait_ge(state_in, 16 * 20)
            m_rows(0)
            m_scores(0)
            for u in range(NU):
                if u + 1 < NU:
                    m_rows(u + 1)
                m_state(u)
                m_values(u)
                if u + 1 < NU:
                    m_scores(u + 1)
                m_update(u)
            pe.wait_ge(m_post_h, 1)
            for i in range(NT):
                if i >= 2:
                    pe.wait_ge(m_rows_act if i % 2 == 0 else m_rows_dve, i // 2)
                for b in range(2):
                    ins = nc.tensor.transpose(bk[4 + i % 2][:, b * P:b * P + P],
                                              hacc[:, i].rearrange("p h v -> p (h v)")[:, b * P:b * P + P], ident[:])
                ins.then_inc(m_rows_full, 1)

            second = iter(range(n_first, len(groups)))

            def s_rows(u, g):
                d, ch = UNITS[u]
                if u >= 1:
                    pe.wait_ge(sL, 2 * (u - 1) + g + 1)
                for r in range(RS):
                    i = d * GW + ch * HS + g * RS + r
                    ins = mm(bk[4 + g][:, r * P:r * P + P], ident[:, i:i + 1].to_broadcast([P, P]), gate(SAR),
                             start=True, stop=True)
                ins.then_inc(sD, 1)

            def s_scores(u):
                d, ch = UNITS[u]
                if u >= 1:
                    pe.wait_ge(sP, 2 * u)
                for g in range(GS):
                    q = slice(HD * g, HD * g + HD)
                    t = slice(cv_tok(ch), cv_tok(ch) + P)
                    ins = mm(bk[6 if g == 0 else 0][:, 0:P], BC[q, 0, t], BC[q, 1, t], start=True, stop=True)
                ins.then_inc(sS, 1)

            def s_state(u):
                d, ch = UNITS[u]
                if u >= 1:
                    pe.wait_ge(sT, u)
                if u >= 2:
                    pe.wait_ge(sH, u - 1)
                mm(bk[2][:, 0:384], BC[:, 1, cv_tok(ch):cv_tok(ch) + P],
                   Hst[:, state_of(u)].rearrange("p g n -> p (g n)"), start=True, stop=True).then_inc(sJ, 1)

            def s_values(u):
                if u >= 1:
                    pe.wait_ge(sY, u)
                pe.wait_ge(sX, u + 1)
                for g in range(GS):
                    pe.wait_ge(sP, 2 * u + g + 1)
                    for r in range(RS):
                        h = g * RS + r
                        ins = mm(bk[7][:, h * HD:h * HD + HD], Ls[:, u % 2, g, r, :], xdt[:, u % 2, h, :],
                                 start=True, stop=True)
                ins.then_inc(sN, 1)

            def s_update(u):
                d, ch = UNITS[u]
                pe.wait_ge(sW, u + 1)
                if u >= 1:
                    pe.wait_ge(sH, u)
                for g in range(GS):
                    ins = mm(bk[1][HD * g:HD * g + HD, 0:RS * HD], brows[:, ch, g * HD:g * HD + HD],
                             wkx[:, u % 2, g * RS:g * RS + RS, :].rearrange("p r v -> p (r v)"), start=True, stop=True)
                ins.then_inc(sU, 1)

            pe.wait_ge(m_rows_act, 5)
            pe.wait_ge(m_rows_dve, 4)
            for g in range(GS):
                s_rows(0, g)
            s_scores(0)
            for u in range(NU):
                if u + 1 < NU:
                    for g in range(GS):
                        s_rows(u + 1, g)
                group(next(second))
                s_state(u)
                s_values(u)
                if u + 1 < NU:
                    s_scores(u + 1)
                s_update(u)
                group(next(second))
            pe.wait_ge(s_y, 1)
            for i in range(NT):
                if i >= 2:
                    pe.wait_ge(s_rows_a if i % 2 == 0 else s_rows_d, i // 2)
                for b in range(3):
                    ins = nc.tensor.transpose(bk[4 + i % 2][:, b * P:b * P + P], yacc[:, i, b * P:b * P + P], ident[:])
                ins.then_inc(s_rows_f, 1)

            def a_scores(a):
                h, j = AU[a]
                q = slice(HD * (h % 2), HD * (h % 2) + HD)
                if a >= 2:
                    pe.wait_ge(aX, a - 1)
                o = 1024 * (a % 2)
                qa = nqT[q, h // 2, (j + 1) * P:(j + 2) * P]
                n = n_local(j)
                k0 = (1 + key_tile(j)) * P
                if j >= 0:
                    mm(psum[:, o:o + 512], qa, nkT[q, h // 2, k0:k0 + 512], start=True, stop=True)
                    if n > 512:
                        mm(psum[:, o + 512:o + n], qa, nkT[q, h // 2, k0 + 512:k0 + n], start=True, stop=True)
                    last = ckT[q, h // 2, :]
                else:
                    last = nkT[q, h // 2, 0:P]
                mm(psum[:, o + n:o + n + P], qa, last, start=True, stop=True).then_inc(aS, 1)

            def a_turned(a):
                _, j = AU[a]
                n = n_local(j)
                pe.wait_ge(aR, a + 1)
                if a >= 1:
                    pe.wait_ge(aPa, turned(a - 1))
                    pe.wait_ge(aPd, a)
                p_ = sc_sb[:, a % 2]
                for m in range(4 if j >= 0 else 0):
                    nc.tensor.transpose(bk[4][:, m * P:m * P + P], p_[:, m * P:m * P + P], ident[:])
                if n > 512:
                    nc.tensor.transpose(bk[5][0:GRID, 0:P], p_[:, 512:n], ident[:])
                nc.tensor.transpose(bk[5][:, P:2 * P], p_[:, n:n + P], ident[:]).then_inc(aT, 1)

            def a_values(a):
                h, j = AU[a]
                v_ = slice(h * HD, h * HD + HD)
                out = bk[6 + a % 2][HD * (h % 2):HD * (h % 2) + HD, 0:P]
                pe.wait_ge(aPa, turned(a))
                pe.wait_ge(aPd, a + 1)
                if a >= 2:
                    pe.wait_ge(aN, a - 1)
                w = pT[:, a % 2]
                for m in range(4 if j >= 0 else 0):
                    mm(out, nv[:, 1 + key_tile(j) + m, v_], w[:, m, :], start=(m == 0), stop=False)
                if n_local(j) > 512:
                    mm(out, nv[0:GRID, 5 + key_tile(j), v_], w[0:GRID, 4, :], start=False, stop=False)
                mm(out, cv[:, v_] if j >= 0 else nv[:, 0, v_], w[:, 5, :], start=(j < 0), stop=True).then_inc(aO, 1)

            pe.wait_ge(cache_in, 32)
            pe.wait_ge(s_rows_a, 5)
            pe.wait_ge(s_rows_d, 4)
            pe.wait_ge(pj_act, evacuated("A", len(groups)))
            a_scores(0)
            for a in range(len(AU)):
                if a + 1 < len(AU):
                    a_scores(a + 1)
                if a >= 1:
                    a_values(a - 1)
                a_turned(a)
            a_values(len(AU) - 1)
            pe.wait_ge(aN, len(AU))

            mods(range(8, 24), G1)
            for j in range(4):
                slab_ready(WOUT + j)
            mix = [mixM[:, 0], mixM[:, 1]] + [mixS[:, b] for b in range(3)] + [mixA[:, b] for b in range(3)]
            def turn_rows(i):
                pe.wait_ge(n2_done, i + 1)
                if i >= 1:
                    pe.wait_ge(h2_act, i)
                    pe.wait_ge(h2_dve, i)
                for k in range(KD):
                    ins = nc.tensor.transpose(psum[:, 512 + k * P:512 + k * P + P], nrow[:, i % 2, k * P:k * P + P], ident[:])
                ins.then_inc(h2_full, 1)

            def router(i):
                pe.wait_ge(h2_act, i + 1)
                pe.wait_ge(h2_dve, i + 1)
                for k in range(KD):
                    ins = mm(bk[0][:, i * NE:i * NE + NE], h2T[:, i % 2, k * P:k * P + P], rw[:, k, :],
                             start=(k == 0), stop=(k == KD - 1))
                ins.then_inc(r_full, 1)

            pe.wait_ge(rw_in, 16)
            for i in range(NT):
                if i >= 2:
                    pe.wait_ge(wo_mul, i - 1)
                for j in range(4):
                    out = bk[4 + 2 * (i % 2) + j // 2][:, (j % 2) * SLAB:(j % 2) * SLAB + SLAB]
                    for k in range(KD):
                        ins = mm(out, mix[k][:, i * P:i * P + P], ring[:, (WOUT + j) % RING, k, :],
                                 start=(k == 0), stop=(k == KD - 1))
                ins.then_inc(wo_full, 1)
                if i >= 2:
                    router(i - 2)
                if i >= 1:
                    turn_rows(i - 1)
            router(NT - 2)
            turn_rows(NT - 1)
            router(NT - 1)
            pe.wait_ge(r_aff, 1)
            for i in range(NT):
                o = 1536 if i == 0 else 512 + (i - 1) * P
                ins = nc.tensor.transpose(psum[0:NE, o:o + P], aff[:, i, :], ident[:])
            ins.then_inc(affT_full, 1)
            pe.wait_ge(k_done, 1)
            for i, t in enumerate((vals, idxf)):
                nc.tensor.transpose(bk[0][:, 16 * i:16 * i + 16], t[0:NE, 0:P], ident[0:NE, 0:NE])
            for i, t in enumerate((vals, idxf)):
                ins = nc.tensor.transpose(bk[0][0:CAPC, 32 + 16 * i:48 + 16 * i], t[0:NE, P:SLOTS], ident[0:NE, 0:NE])
            ins.then_inc(kT_full, 1)

            def x_turn_latent(first, end):
                for k in range(first, end):
                    nc.tensor.transpose(psum[:, 3072 + k * P:3072 + k * P + P], xg[:, k * P:k * P + P], ident[:])

            def x_turn_context():
                for k in range(KD):
                    ins = nc.tensor.transpose(bk[0][:, CAPC * k:CAPC * k + CAPC], xgc[0:CAPC, k * P:k * P + P],
                                              ident[0:CAPC, 0:CAPC])
                ins.then_inc(ex_full, 1)

            pe.wait_ge(k_cols, 2)
            pe.wait_ge(xgl_in, 16)
            pe.wait_ge(xgc_in, 16)
            x_turn_latent(0, KD)
            x_turn_context()
            with pe.Fori(0, NE) as e:
                pe.wait_ge(ex_act, e + 1)
                pe.wait_ge(ex_dve, e + 1)
                for fb in range(KD):
                    a = 2 * (fb // 4)
                    if fb % 4 == 0:
                        pe.wait_ge(w_in_slot[a], (e + 1) * 16)
                        pe.wait_ge(w_in_slot[a + 1], (e + 1) * 16)
                    pe.wait_ge(e_hid, e * KD + (fb + 1))
                    col = slice((fb % 4) * P, (fb % 4) * P + P)
                    for w, bank, done in ((wslot[a], bk[fb % 2], e_h1), (wslot[a + 1], bk[2 + fb % 2], e_h3)):
                        for k in range(KD):
                            ins = mm(bank[:, 0:SLOTS], w[:, k, col], xeT[:, k, :], start=(k == 0), stop=(k == KD - 1))
                        ins.then_inc(done, 1)
                pe.wait_ge(xgl_in, (e + 2) * 16)
                pe.wait_ge(xgc_in, (e + 2) * 16)
                pe.wait_ge(e_yeA, e + 1)
                pe.wait_ge(e_yeD, e + 1)
                x_turn_latent(0, KD - 1)
                pe.wait_ge(e_hid, e * KD + (KD + 2))
                x_turn_latent(KD - 1, KD)
                x_turn_context()
                for db in range(KD):
                    if db % 4 == 0:
                        pe.wait_ge(w_in_slot[4 + db // 4], (e + 1) * 16)
                    pe.wait_ge(e_yA if db % 2 == 0 else e_yD, e * 4 + (db // 2 + 1))
                    for k in range(KD):
                        ins = mm(bk[4 + db % 2][:, 0:SLOTS], wslot[4 + db // 4][:, k, (db % 4) * P:(db % 4) * P + P],
                                 hid[:, k, :], start=(k == 0), stop=(k == KD - 1))
                    ins.then_inc(e_yt, 1)
                pe.wait_ge(ex_act, e + 2)
                pe.wait_ge(ex_dve, e + 2)
                pe.wait_ge(e_yA, e * 4 + 4)
                pe.wait_ge(e_yD, e * 4 + 4)
                for db in range(KD):
                    if db == KD - 2:
                        pe.wait_ge(e_yA, e * 4 + 5)
                        pe.wait_ge(e_yD, e * 4 + 5)
                    nc.tensor.transpose(psum[:, 3072 + db * P:3072 + db * P + P], yT[:, db, 0:P], ident[:])
                for db in range(KD):
                    ins = nc.tensor.transpose(psum[0:CAPC, 2048 + db * P:2048 + db * P + P], yT[:, db, P:SLOTS], ident[:])
                ins.then_inc(e_ty, 1)

        @block.vector
        def _(dve):
            v = nc.vector
            steps = [0]

            def link(ins):
                steps[0] += 1
                ins.then_inc(dve_step, 1)
                dve.wait_ge(dve_step, steps[0])

            def mod_col(m):
                dve.wait_ge(modT_full, m + 1)
                v.tensor_tensor(modcol[:, 2 * m:2 * m + 2, :], bk[3][:, 0:4].rearrange("p (b s) -> p b s", s=2),
                                bc(vcol[:, V_ADAB + 2 * m:V_ADAB + 2 * m + 2], 2), ALU.add).then_inc(modT_done, 1)

            dve.wait_ge(vcol_full, 1)
            v.tensor_copy(vcol[:], bk[0][:, 0:V_END]).then_inc(vcol_done, 1)
            v.tensor_copy(smb[:], bk[0][:, 128:128 + R_END]).then_inc(vcol_done, 1)
            dve.wait_ge(vcol_done, 2)

            for m in range(3):
                mod_col(m)
            dve.wait_ge(sumsq_done, NT)
            v.tensor_scalar(rstd[:, 0, :], sumsq[:, 0, :], 1.0 / D, EPS, ALU.mult, ALU.add).then_inc(msq_done, 1)
            dve.wait_ge(rstd_done, 1)
            for i in range(NT):
                v.tensor_scalar(X[:, i, :], X[:, i, :], rstd[:, 0, i:i + 1], None, ALU.mult).then_inc(xn_done, 1)
                if i in (2, 5, 7):
                    mod_col({2: 3, 5: 4, 7: 5}[i])
            for m in (6, 7):
                mod_col(m)
            dve.wait_ge(modT_done, 8)
            v.scalar_tensor_tensor(gs[0][:], modcol[:, 8:16, :], 1.0, bc(vcol[:, V_N1:V_N1 + KD], 2), ALU.add, ALU.mult)\
                .then_inc(gs_done, 1)
            dve.wait_ge(gs_done, 1)
            for i in range(NT):
                dve.wait_ge(xt_full, i + 1)
                s = min(i, 1)
                for k in range(4, KD):
                    ins = v.tensor_scalar(hT[:, k, i * P:i * P + P], bk[5 + 2 * (i % 2)][:, (k - 4) * P:(k - 3) * P],
                                          gs[0][:, k, s:s + 1], modcol[:, k, s:s + 1], ALU.mult, ALU.add)
                ins.then_inc(xt_dve, 1)

            dve.wait_ge(consts_ready, 5)
            dve.wait_ge(xt_act, NT)

            def evacuate(n):
                kind, _, _, cols, i, target, engine = groups[n]
                if kind == "C":
                    conv(target[1])
                    return
                if engine != "D":
                    return
                q = pe_index[n]
                dve.wait_ge(pj_full, q + 1)
                ps = pj_bank(q)
                if kind == "T" and target[0] == "raw":
                    w = raw[:, target[1] % 2, :]
                    if i == 0:
                        if target[1] >= 2:
                            dve.wait_ge(conv_sum, target[1] - 1)
                        v.tensor_copy(w[:, 1:1 + P], ps[:, 0:P])
                        ins = v.tensor_copy(w[:, 3 + P:3 + 384], ps[:, P:384])
                    else:
                        ins = v.tensor_copy(w[:, 3 + 384 * i:3 + 384 * i + 384], ps[:, 0:384])
                elif kind == "T" and target[0] == "dtT":
                    ins = v.tensor_copy(dtT[0:cols, i * 384:i * 384 + 384], ps[0:cols, 0:384])
                elif kind == "X" and target[0][0] == "dtT":
                    ins = v.tensor_copy(dtr[:, 3 * i:3 * i + 3, :], ps[:, 0:cols].rearrange("p (t h) -> p t h", t=3))
                elif kind == "T":
                    dst, sc = {"qT": (qT, 1.0), "kT": (kT, SCALE), "nqT": (nqT, SCALE), "nkT": (nkT, 1.0)}[target[0]]
                    ins = v.tensor_scalar(dst[:, target[1], i * 384:i * 384 + 384], ps[:, 0:384], sc, None, ALU.mult)
                elif kind == "X":
                    (_, b), (where, _) = target
                    dst = krows if where == "krows" else (xrows if b < 3 else brows)
                    col = b * P if (where == "krows" or b < 3) else 0
                    ins = v.tensor_copy(dst[:, 3 * i:3 * i + 3, col:col + P], ps[:, 0:384].rearrange("p (a b) -> p a b", b=P))
                elif target[0] == "v":
                    ins = v.tensor_copy(v1[:, i, :, 0:HD], ps[:, 0:256].rearrange("p (h v) -> p h v", v=HD))
                elif target[0] == "nv":
                    ins = v.tensor_copy(nv[:, i, target[1]:target[1] + cols], ps[:, 0:cols])
                ins.then_inc(pj_dve, 1)

            def conv(b):
                w, out = raw[:, b % 2, :], conv_out(b)
                dve.wait_ge(conv_mid, b + 1)
                link(v.scalar_tensor_tensor(out, w[:, 0:T + 2], vcol[:, V_CW + b:V_CW + b + 1], out, ALU.mult, ALU.add))
                v.scalar_tensor_tensor(out, w[:, 2:T + 4], vcol[:, V_CW + 10 + b:V_CW + 11 + b], out, ALU.mult, ALU.add)\
                    .then_inc(conv_sum, 1)

            for n in range(n_first):
                evacuate(n)

            dve.wait_ge(pj_act, evacuated("A", n_first))
            dve.wait_ge(pj_dve, evacuated("D", n_first))
            for d in range(NDIR):
                v.tensor_copy(gate(IG, d), G[:, :, 4 * d:4 * d + 4])
                v.tensor_tensor(gate(FL, d), G[:, :, 8 + 4 * d:12 + 4 * d],
                                bmid(smb[:, R_FB + 4 * d:R_FB + 4 * d + 4], NT), ALU.add)
                ins = v.tensor_tensor(gate(DT, d, HS), dtr[:, :, 6 * d:6 * d + 6],
                                      bmid(smb[:, R_DTB + 6 * d:R_DTB + 6 * d + 6], NT), ALU.add)
            ins.then_inc(gm_dve, 1)
            dve.wait_ge(gm_dve, 1)
            dve.wait_ge(gm_act, 3)
            for d in range(NDIR):
                v.scalar_tensor_tensor(gate(F, d), gate(FL, d), 0.0, gate(FE, d), ALU.min, ALU.subtract)
                link(v.scalar_tensor_tensor(gate(DT, d, HS), gate(DT, d, HS), 0.0, gate(DTE, d, HS), ALU.max, ALU.add))
                ins = v.scalar_tensor_tensor(gate(DA, d, HS), gate(DT, d, HS), -1.0,
                                             bmid(smb[:, R_ALOG + 6 * d:R_ALOG + 6 * d + 6], NT), ALU.mult, ALU.mult)
            ins.then_inc(gm_dve, 1)
            dve.wait_ge(gm_full, 1)
            v.tensor_tensor(gate(AC), gate(IG), bk[0][:, 0:P], ALU.subtract).then_inc(gm_dve, 1)
            dve.wait_ge(gm_full, 2)
            v.tensor_copy(gate(SA), bk[2][:, 0:P]).then_inc(gm_dve, 1)
            dve.wait_ge(gm_full, 3)
            link(v.tensor_copy(gate(AR), bk[1][:, 0:P]))
            v.tensor_tensor_scan(gate(CMR)[0:GW, :], gate(AR)[0:GW, :], gate(AR)[0:GW, :], -3e38, ALU.max, ALU.max)
            v.tensor_tensor_scan(gate(CMR)[GW:P, ::-1], gate(AR)[GW:P, ::-1], gate(AR)[GW:P, ::-1], -3e38,
                                 ALU.max, ALU.max).then_inc(gm_dve, 1)
            dve.wait_ge(gm_full, 4)
            v.tensor_copy(gate(SAR), bk[3][:, 0:P]).then_inc(gm_dve, 1)
            dve.wait_ge(gm_full, 5)
            v.tensor_copy(gate(CMC), bk[1][:, P:2 * P]).then_inc(gm_dve, 1)
            dve.wait_ge(gm_full, 6)
            link(v.tensor_copy(gate(MX), bk[1][:, 256:384]))
            btot = bk[0][:, P:2 * P]

            def ctx_cols(ap):
                return ap.rearrange("p (d g) -> p d g", d=NDIR)[:, :, 0:HM]

            v.memset(ctx_cols(gate(MP)), NEG)
            v.scalar_tensor_tensor(ctx_cols(gate(MN)), ctx_cols(gate(MX)), NEG, ctx_cols(btot), ALU.max, ALU.add)
            for d in range(NDIR):
                first = 1 if d == 0 else NT - 1
                v.tensor_copy(gate(MP, d)[:, first, :], smb[:, R_M0 + 4 * d:R_M0 + 4 * d + 4])
                bt = btot[:, d * GW:d * GW + NT * HM].rearrange("p (c h) -> p c h", h=HM)
                for h in range(HM):
                    sl = slice(1, NT) if d == 0 else slice(NT - 1, 0, -1)
                    ins = v.tensor_tensor_scan(gate(MN, d)[:, sl, h], gate(MX, d)[:, sl, h], bt[:, sl, h],
                                               smb[:, R_M0 + 4 * d + h:R_M0 + 4 * d + h + 1], ALU.max, ALU.add)
            link(ins)
            v.tensor_copy(gate(MP, 0)[:, 2:NT, :], gate(MN, 0)[:, 1:NT - 1, :])
            link(v.tensor_copy(gate(MP, 1)[:, 1:NT - 1, :], gate(MN, 1)[:, 2:NT, :]))
            link(v.tensor_tensor(gate(NM), gate(MP), gate(CMC), ALU.max))
            v.tensor_tensor(gate(WINT), gate(MP), gate(NM), ALU.subtract)
            link(v.tensor_tensor(gate(EMT), bk[0][:, 0:P], gate(NM), ALU.add))
            v.tensor_scalar(gate(EMT), gate(EMT), -1.0, None, ALU.mult)
            v.tensor_scalar(gate(NM), gate(NM), -1.0, None, ALU.mult).then_inc(gm_dve, 1)
            link(v.tensor_tensor(gate(FE), btot, gate(MN), ALU.subtract))
            v.tensor_tensor(gate(WKM), gate(AC), gate(FE), ALU.add)
            v.tensor_tensor(gate(DEC), gate(MP), gate(FE), ALU.add)
            v.tensor_copy(gate(SEA), gate(SA))
            v.tensor_copy(gate(SEL), bk[2][:, P:2 * P])
            v.tensor_tensor(gate(SWK), bk[2][:, P:2 * P], gate(SA), ALU.subtract).then_inc(gm_dve, 1)
            dve.wait_ge(gm_full, 7)
            v.tensor_copy(gate(NMR), bk[1][:, 384:512]).then_inc(gm_dve, 1)
            dve.wait_ge(gm_act, 4)
            for d in range(NDIR):
                src = gate(DEC)[:, d * GW:d * GW + NT * HM].rearrange("p (n e) -> p n e", e=2)
                for e in range(2):
                    v.tensor_copy(dec2[HD * e:HD * e + HD, d, :], src[HD * e:HD * e + HD, :, e])
            v.tensor_tensor(gate(SWK), gate(SWK), gate(DT), ALU.mult).then_inc(gm_dve, 1)

            def m_log(u):
                d, ch = UNITS[u]
                dve.wait_ge(mD, u + 1)
                if u >= 2:
                    dve.wait_ge(mN, u - 1)
                for h in range(HM):
                    ins = v.scalar_tensor_tensor(Lm[:, u % 2, h % 2, h // 2, :], bk[4 + u % 2][:, h * P:h * P + P],
                                                 gcol(AC, d, ch, h), mask[d][:], ALU.add, ALU.min)
                ins.then_inc(mL, 1)

            def m_weights(u):
                dve.wait_ge(mE, u + 1)
                dve.wait_ge(mS, u + 1)
                for e in range(2):
                    w = Lm[:, u % 2, e].rearrange("p j t -> p (j t)")
                    ins = v.tensor_tensor(w, w, bk[6 if e == 0 else 0][:, 0:2 * P], ALU.mult)
                ins.then_inc(mP, 1)

            def m_finish(u):
                d, ch = UNITS[u]
                inter, nu = bk[2 + u % 2], bk[7 if u % 2 == 0 else 1]
                nm, rc, emt = num[:, u % 2], rec[:, u % 2], gate(EMT, d)[:, ch, :]
                dve.wait_ge(mJ, u + 1)
                v.tensor_tensor(nm, inter[:, 0:260].rearrange("p (h v) -> p h v", v=HD + 1),
                                bc(gate(WINT, d)[:, ch, :], HD + 1), ALU.mult)
                dve.wait_ge(mU, u + 1)
                st = state_of(u)
                for e in range(2):
                    q = slice(HD * e, HD * e + HD)
                    for j in range(2):
                        ins = v.scalar_tensor_tensor(Cst[q, st, e, j, :], Cst[q, st, e, j, :],
                                                     dec2[q, d, 2 * ch + j:2 * ch + j + 1],
                                                     nu[q, 260 + 65 * j:325 + 65 * j], ALU.mult, ALU.add)
                ins.then_inc(mC, 1)
                dve.wait_ge(mC, u + 1)
                v.tensor_tensor(nm, nm, nu[:, 0:260].rearrange("p (h v) -> p h v", v=HD + 1), ALU.add).then_inc(mH, 1)
                dve.wait_ge(mH, u + 1)
                link(v.tensor_tensor(rc, nm[:, :, HD], emt, ALU.max))
                link(v.scalar_tensor_tensor(rc, nm[:, :, HD], -1.0, rc, ALU.mult, ALU.max))
                link(v.reciprocal(rc, rc))
                if first_visit(u):
                    ins = v.tensor_tensor(hacc[:, ch], nm[:, :, 0:HD], bc(rc, HD), ALU.mult)
                else:
                    link(v.tensor_tensor(htmp, nm[:, :, 0:HD], bc(rc, HD), ALU.mult))
                    ins = v.tensor_tensor(hacc[:, ch], hacc[:, ch], htmp, ALU.add)
                ins.then_inc(m_h_done, 1)
                dve.wait_ge(m_h_done, u + 1)

            m_log(0)
            for u in range(NU):
                if u + 1 < NU:
                    m_log(u + 1)
                m_weights(u)
                if u >= 1:
                    m_finish(u - 1)
            m_finish(NU - 1)
            dve.wait_ge(sumsq_done, SQ_M + 1)
            link(v.tensor_reduce(small[:, 0, 0:36], SQ, AX, ALU.add))
            v.tensor_scalar(small[:, 0, 0:36], small[:, 0, 0:36], 1.0 / HD, EPS, ALU.mult, ALU.add).then_inc(msq_done, 1)
            dve.wait_ge(rstd_done, RS_M + 1)
            h36 = hacc.rearrange("p c h v -> p (c h) v")
            link(v.tensor_tensor(h36, h36, bc(small[:, 0, 0:36], HD), ALU.mult))
            dve.wait_ge(mo_in, 16)
            hrow = hacc.rearrange("p c h v -> p c (h v)")
            v.tensor_tensor(hrow, hrow, mo, ALU.mult).then_inc(m_post_h, 1)
            for i in range(1, NT, 2):
                dve.wait_ge(m_rows_full, i + 1)
                for b in range(2):
                    ins = v.tensor_scalar(mixM[:, b, i * P:i * P + P], bk[4 + i % 2][:, b * P:b * P + P],
                                          vcol[:, V_MG + b:V_MG + b + 1], None, ALU.mult)
                ins.then_inc(m_rows_dve, 1)

            def s_log(u, g):
                d, ch = UNITS[u]
                dve.wait_ge(sD, 2 * u + g + 1)
                if u >= 2:
                    dve.wait_ge(sN, u - 1)
                for r in range(RS):
                    ins = v.scalar_tensor_tensor(Ls[:, u % 2, g, r, :], bk[4 + g][:, r * P:r * P + P],
                                                 gcol(SA, d, ch, g * RS + r, HS), mask[d][:], ALU.subtract, ALU.min)
                ins.then_inc(sL, 1)

            def s_weights(u, g):
                dve.wait_ge(sE, 2 * u + g + 1)
                dve.wait_ge(sS, u + 1)
                w = Ls[:, u % 2, g]
                v.tensor_tensor(w, w, bmid(bk[6 if g == 0 else 0][:, 0:P], RS), ALU.mult).then_inc(sP, 1)

            def s_finish(u):
                d, ch = UNITS[u]
                y3 = yacc[:, ch].rearrange("p (h v) -> p h v", v=HD)
                dve.wait_ge(sJ, u + 1)
                v.tensor_tensor(yint, bk[2][:, 0:384].rearrange("p (h v) -> p h v", v=HD),
                                bc(gate(SEA, d, HS)[:, ch, :], HD), ALU.mult).then_inc(sT, 1)
                dve.wait_ge(sU, u + 1)
                dve.wait_ge(sHT, u + 1)
                for g in range(GS):
                    q = slice(HD * g, HD * g + HD)
                    ins = v.tensor_tensor(Hst[q, state_of(u), g, :], hs[q, :], bk[1][q, 0:RS * HD], ALU.add)
                ins.then_inc(sH, 1)
                dve.wait_ge(sH, u + 1)
                link(v.tensor_tensor(y3, y3, yint, ALU.add))
                v.tensor_tensor(y3, y3, bk[7][:, 0:384].rearrange("p (h v) -> p h v", v=HD), ALU.add).then_inc(sY, 1)
                dve.wait_ge(sY, u + 1)

            dve.wait_ge(m_rows_full, NT)
            dve.wait_ge(y_init, NT)
            for g in range(GS):
                s_log(0, g)
            for u in range(NU):
                if u + 1 < NU:
                    for g in range(GS):
                        s_log(u + 1, g)
                for g in range(GS):
                    s_weights(u, g)
                if u >= 1:
                    s_finish(u - 1)
            s_finish(NU - 1)
            dve.wait_ge(z_in, 16)
            link(v.tensor_tensor(yacc, yacc, z, ALU.mult))
            dve.sem_inc(yz, 1)
            dve.wait_ge(sumsq_done, SQ_S + NT)
            v.tensor_scalar(rstd[:, 1, :], sumsq[:, 1, :], 1.0 / 384, EPS, ALU.mult, ALU.add).then_inc(msq_done, 1)
            dve.wait_ge(rstd_done, RS_S + 1)
            v.tensor_tensor(yacc, yacc, bc(rstd[:, 1, :], 384), ALU.mult).then_inc(s_y, 1)
            for i in range(1, NT, 2):
                dve.wait_ge(s_rows_f, i + 1)
                for b in range(3):
                    ins = v.tensor_scalar(mixS[:, b, i * P:i * P + P], bk[4 + i % 2][:, b * P:b * P + P],
                                          vcol[:, V_SG + b:V_SG + b + 1], None, ALU.mult)
                ins.then_inc(s_rows_d, 1)

            def a_bias(a):
                h, j = AU[a]
                n, o = n_local(j), 1024 * (a % 2)
                dve.wait_ge(aS, a + 1)
                if a >= 2:
                    dve.wait_ge(aT, a - 1)
                s_ = sc_sb[:, a % 2]
                if j >= 0:
                    dve.wait_ge(tab_done, h + 1)
                    if n > 512:
                        t = ti[:, h % 2]
                    else:
                        first = {0: 6, 1: 4, 6: 2, 7: 0}[j]
                        t = tb[:, h % 2, first:first + 8, :]
                    v.tensor_tensor(s_[:, 0:n].rearrange("p (a b) -> p a b", b=GRID),
                                    psum[:, o:o + n].rearrange("p (a b) -> p a b", b=GRID), t[:, :, ::-1], ALU.add)
                v.tensor_copy(s_[:, n:n + P], psum[:, o + n:o + n + P]).then_inc(aX, 1)
                dve.wait_ge(aX, a + 1)
                link(v.tensor_reduce(nmax[:, a:a + 1], s_[:, 0:n + P], AX, ALU.max))
                v.tensor_scalar(nmax[:, a:a + 1], nmax[:, a:a + 1], -1.0, None, ALU.mult).then_inc(aM, 1)

            def a_turn(a):
                dve.wait_ge(aT, a + 1)
                if a >= 2:
                    dve.wait_ge(aO, a - 1)
                if n_local(AU[a][1]) > 512:
                    v.tensor_copy(pT[0:GRID, a % 2, 4, :], bk[5][0:GRID, 0:P])
                v.tensor_copy(pT[:, a % 2, 5, :], bk[5][:, P:2 * P]).then_inc(aPd, 1)

            def a_scale(a):
                h, j = AU[a]
                dve.wait_ge(aE, a + 1)
                link(v.reciprocal(rsum[:, a:a + 1], ssum[:, a:a + 1]))
                p_ = sc_sb[:, a % 2, 0:n_local(j) + P]
                v.tensor_scalar(p_, p_, rsum[:, a:a + 1], None, ALU.mult).then_inc(aR, 1)

            def a_out(a):
                h, j = AU[a]
                q = slice(HD * (h % 2), HD * (h % 2) + HD)
                dve.wait_ge(aO, a + 1)
                v.tensor_copy(mixA[q, h // 2, (j + 1) * P:(j + 2) * P], bk[6 + a % 2][q, 0:P]).then_inc(aN, 1)

            a_bias(0)
            a_scale(0)
            for a in range(len(AU)):
                if a + 1 < len(AU):
                    a_bias(a + 1)
                    a_scale(a + 1)
                a_turn(a)
                if a >= 1:
                    a_out(a - 1)
            a_out(len(AU) - 1)

            for m in range(8, 24):
                if m in gates:
                    i = gates.index(m)
                    dve.wait_ge(modT_full, m + 1)
                    gb = g1b if i < 4 else g2b
                    v.tensor_copy(gb[:, :, (i % 4) * SLAB:(i % 4) * SLAB + SLAB],
                                  bk[3].rearrange("p (s n) -> p s n", s=2)).then_inc(modT_done, 1)
                else:
                    mod_col(m)
            dve.wait_ge(modT_done, 24)
            v.scalar_tensor_tensor(gs[1][:], modcol[:, 32:40, :], 1.0, bc(vcol[:, V_N2:V_N2 + KD], 2), ALU.add, ALU.mult)\
                .then_inc(gs_done, 1)
            dve.wait_ge(gs_done, 2)
            for i in range(NT + 1):
                if i < NT:
                    dve.wait_ge(wo_full, i + 1)
                    if i >= 2:
                        dve.wait_ge(x1_done, i - 1)
                    o = 2048 + 1024 * (i % 2)
                    v.tensor_tensor(tw[:, i % 2, :], psum[:, o:o + D], g1b[:, min(i, 1), :], ALU.mult).then_inc(wo_mul, 1)
                if i >= 1:
                    q = i - 1
                    dve.wait_ge(h2_full, q + 1)
                    if q >= 2:
                        dve.wait_ge(r_full, q - 1)
                    s = min(q, 1)
                    for k in range(4, KD):
                        ins = v.tensor_scalar(h2T[:, q % 2, k * P:k * P + P], bk[2][:, (k - 4) * P:(k - 3) * P],
                                              gs[1][:, k, s:s + 1], modcol[:, 24 + k, s:s + 1], ALU.mult, ALU.add)
                    ins.then_inc(h2_dve, 1)
                if i < NT:
                    dve.wait_ge(sumsq_done, SQ_N2 + i + 1)
                    v.tensor_scalar(rstd[:, 2, i:i + 1], sumsq[:, 2, i:i + 1], 1.0 / D, EPS, ALU.mult, ALU.add)\
                        .then_inc(msq_done, 1)
                    dve.wait_ge(rstd_done, RS_N2 + i + 1)
                    if i >= 2:
                        dve.wait_ge(n2_out[i % 2], 16 * (i // 2))
                        dve.wait_ge(h2_full, i - 1)
                    v.tensor_scalar(nrow[:, i % 2, :], x1[:, i, :], rstd[:, 2, i:i + 1], None, ALU.mult).then_inc(n2_done, 1)
            dve.wait_ge(r_full, NT)
            lps = bk[0][:, 0:NT * NE].rearrange("p (t e) -> p t e", e=NE)
            link(v.tensor_reduce(smx, lps, AX, ALU.max))
            v.tensor_tensor(lg, lps, bc(smx, NE), ALU.subtract).then_inc(r_sub, 1)
            dve.wait_ge(r_exp, 1)
            link(v.tensor_reduce(ssm, aff, AX, ALU.add))
            link(v.reciprocal(ssm, ssm))
            v.tensor_tensor(aff, aff, bc(ssm, NE), ALU.mult).then_inc(r_aff, 1)
            dve.wait_ge(affT_full, 1)
            v.tensor_copy(affT[0:NE, 0:NL * P], psum[0:NE, 512:1536])
            link(v.tensor_copy(affT[0:NE, NL * P:T], psum[0:NE, 1536:1664]))
            for a, b, o, cap in ((0, NL * P, 0, CAPL), (NL * P, T, P, CAPC)):
                for r in range(o, o + cap, 8):
                    link(v.max(vals[0:NE, r:r + 8], affT[0:NE, a:b]))
                    link(v.max_index(idxu[0:NE, r:r + 8], vals[0:NE, r:r + 8], affT[0:NE, a:b]))
                    if r + 8 < o + cap:
                        link(v.match_replace(affT[0:NE, a:b], vals[0:NE, r:r + 8], affT[0:NE, a:b], -1.0))
            v.tensor_copy(idxf[0:NE, :], idxu[0:NE, :]).then_inc(k_done, 1)
            dve.wait_ge(kT_full, 1)
            v.tensor_copy(gl, bk[0][:, 0:16])
            v.tensor_copy(gc[0:CAPC, :], bk[0][0:CAPC, 32:48])
            v.tensor_copy(il[:, 0:NE], bk[0][:, 16:32])
            v.tensor_copy(ic[0:CAPC, 0:NE], bk[0][0:CAPC, 48:64])
            v.tensor_copy(il[:, NE:NE + 1], bk[0][:, 31:32])
            v.tensor_copy(ic[0:CAPC, NE:NE + 1], bk[0][0:CAPC, 63:64])
            v.tensor_copy(icur[:, 0:1], bk[0][:, 16:17])
            v.tensor_copy(icur[0:CAPC, 1:2], bk[0][0:CAPC, 48:49]).then_inc(k_cols, 1)
            dve.wait_ge(k_cols, 1)

            def x_evac():
                for k in range(4, KD):
                    v.tensor_scalar(xeT[:, k, 0:P], bk[7][:, (k - 4) * P:(k - 3) * P], gs[1][:, k, 1:2],
                                    modcol[:, 24 + k, 1:2], ALU.mult, ALU.add)
                c3 = bk[0][:, 0:KD * CAPC].rearrange("p (k s) -> p k s", s=CAPC)
                v.tensor_tensor(xeT[:, :, P:SLOTS], c3, bc(gs[1][:, :, 0], CAPC), ALU.mult).then_inc(xc_mid, 1)

            def x_shift():
                v.tensor_tensor(xeT[:, :, P:SLOTS], xeT[:, :, P:SLOTS], bc(modcol[:, 24:32, 0], CAPC), ALU.add)\
                    .then_inc(ex_dve, 1)

            dve.sem_inc(k_cols, 1)
            dve.wait_ge(ex_full, 1)
            x_evac()
            dve.wait_ge(xc_mid, 1)
            x_shift()
            dve.sem_inc(e_hid, 2)
            dve.sem_inc(e_yD, 1)
            dve.sem_inc(e_yeD, 1)
            with dve.Fori(0, NE) as e:
                dve.wait_ge(e_yeA, e + 1)
                dve.wait_ge(e_yeD, e + 1)
                v.tensor_copy(gcur[:, 0:1], gl[:, bass.ds(e, 1)])
                v.tensor_copy(gcur[0:CAPC, 1:2], gc[0:CAPC, bass.ds(e, 1)]).then_inc(gcur_set, 1)
                for fb in range(KD):
                    dve.wait_ge(e_sil, e * KD + (fb + 1))
                    dve.wait_ge(e_h3, e * KD + (fb + 1))
                    v.tensor_tensor(hid[:, fb, :], sil[:, fb % 2, :], bk[2 + fb % 2][:, 0:SLOTS], ALU.mult)\
                        .then_inc(e_hid, 1)
                dve.wait_ge(ex_full, e + 2)
                x_evac()
                dve.wait_ge(xc_mid, e + 2)
                x_shift()
                for db in range(1, KD, 2):
                    dve.wait_ge(e_yt, e * KD + (db + 1))
                    v.tensor_copy(yT[:, db, :], bk[5][:, 0:SLOTS]).then_inc(e_yD, 1)
                dve.wait_ge(e_ty, e + 1)
                dve.wait_ge(e_free, e + 1)
                dve.wait_ge(gcur_set, e + 1)
                v.tensor_scalar(ye[:, 512:1024], bk[7], gcur[:, 0:1], None, ALU.mult)
                v.tensor_scalar(yec[0:CAPC, :], psum[0:CAPC, 2048:3072], gcur[0:CAPC, 1:2], None, ALU.mult)\
                    .then_inc(e_yeD, 1)

            dve.wait_ge(fg_in, 16)
            for i in range(NT + 4):
                if i < NT:
                    dve.wait_ge(x_in[i // 3], 96)
                    v.tensor_tensor(y9[:, i, :], y9[:, i, :], g2b[:, min(i, 1), :], ALU.mult).then_inc(f_mul, 1)
                if 3 <= i < NT + 3:
                    q = i - 3
                    dve.wait_ge(sumsq_done, SQ_F + q + 1)
                    v.tensor_scalar(rstd[:, 3, q:q + 1], sumsq[:, 3, q:q + 1], 1.0 / D, EPS, ALU.mult, ALU.add)\
                        .then_inc(msq_done, 1)
                if i >= 4:
                    q = i - 4
                    dve.wait_ge(rstd_done, RS_F + q + 1)
                    v.scalar_tensor_tensor(y9[:, q, :], y9[:, q, :], rstd[:, 3, q:q + 1], fgb, ALU.mult, ALU.mult)\
                        .then_inc(f_y, 1)




_SHAPES = [(P, D), (NL * P, D), (384, P), (P, 384), (2, HM, HD, HD), (2, HM, HD), (2, HM), (2, P, RS * HD)]


def kernel(x_prompt, x_sample, cache_na_k, cache_na_v, state_mlstm_c, state_mlstm_n, state_mlstm_m, state_ssm, c, c_ctx,
           ada_w, ada_b, norm1_g, norm2_g, w_in, mlstm_f_bias, mlstm_norm_g, conv_w, conv_b, ssm_dt_bias, ssm_a_log, ssm_d,
           ssm_norm_g, na_rpb, w_out, router_w, exp_w1, exp_w3, exp_w2, final_g):
    import numpy as _np
    import concourse.bacc as _bacc
    from concourse.bass_utils import run_bass_kernel_spmd as _run

    rows = na_rpb[..., ::-1].reshape(-1)
    rpb = _np.zeros(rows.shape[0] + 128, rows.dtype)
    rpb[64:-64] = rows
    ins = [
        ("x_prompt", x_prompt[0]), ("x_sample", x_sample[0]),
        ("cacheT_k", cache_na_k[0, 0].reshape(P, -1).T), ("cache_v", cache_na_v[0, 0].reshape(P, -1)),
        ("state_c", state_mlstm_c[0, 0]), ("state_n", state_mlstm_n[0, 0]), ("state_m", state_mlstm_m.reshape(-1)),
        ("state_sT", state_ssm[0, 0].reshape(2, GS, RS, HD, HD).transpose(0, 1, 4, 2, 3).reshape(2, P, RS * HD)),
        ("c", c[0]), ("c_ctx", c_ctx), ("ada_w", ada_w[0]), ("ada_b", ada_b[0]), ("norm1_g", norm1_g[0]),
        ("norm2_g", norm2_g[0]), ("w_in", w_in[0]), ("f_bias", mlstm_f_bias.reshape(-1)), ("m_norm_g", mlstm_norm_g[0]),
        ("conv_w", conv_w.reshape(-1)), ("conv_b", conv_b[0]), ("dt_bias", ssm_dt_bias.reshape(-1)),
        ("a_log", ssm_a_log.reshape(-1)), ("d_skip", ssm_d[0]), ("s_norm_g", ssm_norm_g[0]), ("rpb_pad", rpb),
        ("w_out", w_out[0]), ("router_w", router_w[0]), ("exp_w1", exp_w1[0]), ("exp_w3", exp_w3[0]),
        ("exp_w2", exp_w2[0]), ("final_g", final_g),
    ]
    nc = _bacc.Bacc("TRN2", target_bir_lowering=False, num_devices=1)
    arrays = {f"in_{n}": _np.ascontiguousarray(a) for n, a in ins}
    args = [nc.dram_tensor(n, a.shape, mybir.dt.from_np(a.dtype), kind="ExternalInput").ap() for n, a in arrays.items()]
    args += [nc.dram_tensor(f"out_{i}", s, F32, kind="ExternalOutput").ap() for i, s in enumerate(_SHAPES)]
    hybrid_layer(nc, *args)
    r = _run(nc, [arrays], core_ids=[0])
    y_p, y_s, kT, v, mc, mn, mm_, sT = (r.results[0][f"out_{i}"] for i in range(len(_SHAPES)))
    return (y_p.reshape(1, P, D), y_s.reshape(1, NL * P, D), kT.T.reshape(1, 1, P, HN, HD), v.reshape(1, 1, P, HN, HD),
            mc.reshape(1, 1, 2, HM, HD, HD), mn.reshape(1, 1, 2, HM, HD), mm_.reshape(1, 1, 2, HM),
            sT.reshape(2, GS, HD, RS, HD).transpose(0, 1, 3, 4, 2).reshape(1, 1, 2, HS, HD, HD))
```
